# Optimizing a Trainium2 kernel written in Bass

```python
import math
import jax, jax.numpy as jnp
from jax import lax
import numpy as np

D_MODEL = 1024
BATCH = 1
SEQ = 1024
DEPTH = 1

ATTN_HEADS = 8
ATTN_KV_HEADS = 2
ATTN_HEAD_DIM = 64
WINDOW = 128
ATTN_BLOCK = 128
ROPE_THETA = 10000.0
DN_HEADS = 4
DN_HEAD_DIM = 128
DN_CONV = 4
DN_CHUNK = 64
ATTN_Q = ATTN_HEADS * ATTN_HEAD_DIM
ATTN_KV = ATTN_KV_HEADS * ATTN_HEAD_DIM
DN_DIM = DN_HEADS * DN_HEAD_DIM
MIX_WIDTH = ATTN_Q + DN_DIM
SPLITS = (ATTN_Q, ATTN_KV, ATTN_KV, DN_DIM, DN_DIM, DN_DIM, DN_HEADS, DN_HEADS, DN_DIM)
IN_WIDTH = ATTN_Q + 2 * ATTN_KV + 4 * DN_DIM + 2 * DN_HEADS
PEER_HEADS = 8
PEER_N_KEYS = 128
PEER_N_EXPERTS = PEER_N_KEYS * PEER_N_KEYS
PEER_QUERY_DIM = 256
PEER_TOPK = 16
PEER_TOKEN_BLOCK = 128
DEEPNORM_ALPHA = (2.0 * DEPTH) ** 0.25
DEEPNORM_BETA = (8.0 * DEPTH) ** -0.25
LN_EPS = 1e-5
RMS_EPS = 1e-6
L2_EPS = 1e-6
NEG_INF = -1e30

kernel_name = 'hymba_swa_sink_gdn_peer_deepnorm'

def layer_norm(x, g, b):
    xf = x.astype(jnp.float32)
    mu = jnp.mean(xf, axis=-1, keepdims=True)
    var = jnp.mean(jnp.square(xf - mu), axis=-1, keepdims=True)
    return ((xf - mu) * lax.rsqrt(var + LN_EPS) * g.astype(jnp.float32) + b.astype(jnp.float32)).astype(x.dtype)

def rope(x, positions):
    half = x.shape[-1] // 2
    inv_freq = ROPE_THETA ** (-jnp.arange(half, dtype=jnp.float32) / half)
    ang = positions.astype(jnp.float32)[..., None] * inv_freq
    cos = jnp.cos(ang)[:, :, None, :]
    sin = jnp.sin(ang)[:, :, None, :]
    xf = x.astype(jnp.float32)
    x1, x2 = xf[..., :half], xf[..., half:]
    return jnp.concatenate([x1 * cos - x2 * sin, x2 * cos + x1 * sin], axis=-1).astype(x.dtype)

def sliding_window_sink_attention(q, k, v, sinks):
    B, T, _, hd = q.shape
    L = ATTN_BLOCK
    nb = T // L
    G = ATTN_HEADS // ATTN_KV_HEADS
    qb = q.reshape(B, nb, L, ATTN_KV_HEADS, G, hd)

    def with_prev(a):
        ab = a.reshape(B, nb, L, ATTN_KV_HEADS, hd)
        prev = jnp.pad(ab[:, :-1], ((0, 0), (1, 0), (0, 0), (0, 0), (0, 0)))
        return jnp.concatenate([prev, ab], axis=2)

    kb, vb = with_prev(k), with_prev(v)
    s = jnp.einsum('bnqhgd,bnkhd->bnhgqk', qb, kb, preferred_element_type=jnp.float32) * (hd ** -0.5)
    blk = jnp.arange(nb)[:, None] * L
    qpos = blk + jnp.arange(L)[None, :]
    kpos = blk - L + jnp.arange(2 * L)[None, :]
    delta = qpos[:, :, None] - kpos[:, None, :]
    allowed = (delta >= 0) & (delta < WINDOW) & (kpos[:, None, :] >= 0)
    s = jnp.where(allowed[None, :, None, None], s, NEG_INF)
    sink_col = jnp.broadcast_to(
        sinks.astype(jnp.float32).reshape(1, 1, ATTN_KV_HEADS, G, 1, 1), s.shape[:-1] + (1,))
    p = jax.nn.softmax(jnp.concatenate([s, sink_col], axis=-1), axis=-1)[..., :-1]
    o = jnp.einsum('bnhgqk,bnkhd->bnqhgd', p.astype(v.dtype), vb)
    return o.reshape(B, T, ATTN_HEADS * hd)

def causal_short_conv(x, w):
    K, C = w.shape
    y = lax.conv_general_dilated(
        x, w[:, None, :].astype(x.dtype), window_strides=(1,), padding=[(K - 1, 0)],
        dimension_numbers=('NWC', 'WIO', 'NWC'), feature_group_count=C)
    return jax.nn.silu(y)

def gated_delta_rule(q, k, v, g, beta):
    B, H, T, dk = q.shape
    dv = v.shape[-1]
    C = DN_CHUNK
    N = T // C
    q = q * (dk ** -0.5)
    q, k, v = (a.reshape(B, H, N, C, a.shape[-1]) for a in (q, k, v))
    g, beta = (a.reshape(B, H, N, C) for a in (g, beta))
    gc = jnp.cumsum(g, axis=-1)
    causal = jnp.tril(jnp.ones((C, C), dtype=bool))
    strict = jnp.tril(jnp.ones((C, C), dtype=bool), -1)
    diff = gc[..., :, None] - gc[..., None, :]
    decay = jnp.where(causal, jnp.exp(jnp.where(causal, diff, 0.0)), 0.0)
    k_beta = k * beta[..., None]
    a_mat = jnp.where(strict, jnp.einsum('bhnid,bhnjd->bhnij', k_beta, k) * decay, 0.0)
    eye = jnp.eye(C, dtype=q.dtype)
    rhs = jnp.concatenate([v * beta[..., None], k_beta * jnp.exp(gc)[..., None]], axis=-1)
    sol = lax.linalg.triangular_solve(eye + a_mat, rhs, left_side=True, lower=True, unit_diagonal=True)
    u, w = sol[..., :dv], sol[..., dv:]
    qk = jnp.einsum('bhnid,bhnjd->bhnij', q, k) * decay
    q_dec = q * jnp.exp(gc)[..., None]
    k_dec = k * jnp.exp(gc[..., -1:] - gc)[..., None]
    g_last = jnp.exp(gc[..., -1])

    def step(S, xs):
        qk_i, qd_i, kd_i, u_i, w_i, gl_i = xs
        v_new = u_i - jnp.einsum('bhid,bhde->bhie', w_i, S)
        o_i = jnp.einsum('bhid,bhde->bhie', qd_i, S) + jnp.einsum('bhij,bhje->bhie', qk_i, v_new)
        S = S * gl_i[..., None, None] + jnp.einsum('bhid,bhie->bhde', kd_i, v_new)
        return S, o_i

    xs = tuple(jnp.moveaxis(a, 2, 0) for a in (qk, q_dec, k_dec, u, w, g_last))
    S0 = jnp.zeros((B, H, dk, dv), q.dtype)
    _, o = lax.scan(step, S0, xs)
    return jnp.moveaxis(o, 0, 2).reshape(B, H, T, dv)

def l2_normalize(a):
    return a * lax.rsqrt(jnp.sum(jnp.square(a), axis=-1, keepdims=True) + L2_EPS)

def hybrid_mixer(x, positions, w_in, attn_sinks, conv_w, a_log, dt_bias, dn_norm_g, w_out):
    B, T, _ = x.shape
    proj = x @ w_in
    offsets = np.cumsum(SPLITS)[:-1].tolist()
    q_a, k_a, v_a, q_d, k_d, v_d, b_d, a_d, z_d = jnp.split(proj, offsets, axis=-1)

    q_a = rope(q_a.reshape(B, T, ATTN_HEADS, ATTN_HEAD_DIM), positions)
    k_a = rope(k_a.reshape(B, T, ATTN_KV_HEADS, ATTN_HEAD_DIM), positions)
    v_a = v_a.reshape(B, T, ATTN_KV_HEADS, ATTN_HEAD_DIM)
    o_attn = sliding_window_sink_attention(q_a, k_a, v_a, attn_sinks)

    qkv = causal_short_conv(jnp.concatenate([q_d, k_d, v_d], axis=-1), conv_w).astype(jnp.float32)
    q_d, k_d, v_d = jnp.split(qkv, 3, axis=-1)
    to_heads = lambda a: jnp.transpose(a.reshape(B, T, DN_HEADS, DN_HEAD_DIM), (0, 2, 1, 3))
    q_d, k_d, v_d = l2_normalize(to_heads(q_d)), l2_normalize(to_heads(k_d)), to_heads(v_d)
    beta = jnp.transpose(jax.nn.sigmoid(b_d.astype(jnp.float32)), (0, 2, 1))
    g = -jnp.exp(a_log.astype(jnp.float32)) * jax.nn.softplus(
        a_d.astype(jnp.float32) + dt_bias.astype(jnp.float32))
    g = jnp.transpose(g, (0, 2, 1))
    o_dn = jnp.transpose(gated_delta_rule(q_d, k_d, v_d, g, beta), (0, 2, 1, 3))
    o_dn = o_dn * lax.rsqrt(jnp.mean(jnp.square(o_dn), axis=-1, keepdims=True) + RMS_EPS)
    o_dn = o_dn * dn_norm_g.astype(jnp.float32) * jax.nn.silu(
        z_d.reshape(B, T, DN_HEADS, DN_HEAD_DIM).astype(jnp.float32))
    o_dn = o_dn.reshape(B, T, DN_DIM).astype(x.dtype)

    return jnp.concatenate([o_attn, o_dn], axis=-1) @ w_out

def peer_ffn(x, w_query, sub_keys, expert_u, expert_v):
    B, T, D = x.shape
    L = PEER_TOKEN_BLOCK
    K = PEER_TOPK
    xt = x.reshape(-1, L, D)

    def one_block(xb):
        q = (xb @ w_query).reshape(L, PEER_HEADS, 2, PEER_QUERY_DIM // 2)
        s = jnp.einsum('lhpd,hpkd->lhpk', q, sub_keys, preferred_element_type=jnp.float32)
        vals, idx = lax.top_k(s, K)
        cand = (vals[..., 0, :, None] + vals[..., 1, None, :]).reshape(L, PEER_HEADS, K * K)
        cidx = (idx[..., 0, :, None] * PEER_N_KEYS + idx[..., 1, None, :]).reshape(L, PEER_HEADS, K * K)
        best, pos = lax.top_k(cand, K)
        expert = jnp.take_along_axis(cidx, pos, axis=-1)
        gate = jax.nn.softmax(best, axis=-1)
        u = expert_u[expert]
        v = expert_v[expert]
        h = jax.nn.gelu(jnp.einsum('ld,lhkd->lhk', xb, u), approximate=False)
        return jnp.einsum('lhk,lhkd->ld', (h * gate).astype(xb.dtype), v)

    return lax.map(one_block, xt).reshape(B, T, D)

def setup_inputs(seed: int = 0) -> dict:
    key = jax.random.key(seed)
    ks = jax.random.split(key, 20)
    f32 = jnp.float32
    nrm = lambda k, shape, std: jax.random.normal(k, shape, f32) * std
    x = nrm(ks[0], (BATCH, SEQ, D_MODEL), 1.0)
    positions = jnp.broadcast_to(jnp.arange(SEQ, dtype=jnp.int32)[None, :], (BATCH, SEQ))
    w_in = nrm(ks[1], (D_MODEL, IN_WIDTH), D_MODEL ** -0.5)
    attn_sinks = nrm(ks[2], (ATTN_HEADS,), 0.5)
    conv_w = nrm(ks[3], (DN_CONV, 3 * DN_DIM), DN_CONV ** -0.5)
    a_log = jnp.log(jax.random.uniform(ks[4], (DN_HEADS,), f32, 1.0, 16.0))
    dt = jnp.exp(jax.random.uniform(ks[5], (DN_HEADS,), f32, math.log(1e-3), math.log(1e-1)))
    dt_bias = dt + jnp.log(-jnp.expm1(-dt))
    dn_norm_g = 1.0 + nrm(ks[6], (DN_HEAD_DIM,), 0.02)
    w_out = nrm(ks[7], (MIX_WIDTH, D_MODEL), MIX_WIDTH ** -0.5 * DEEPNORM_BETA)
    ln1_g = 1.0 + nrm(ks[8], (D_MODEL,), 0.02)
    ln1_b = nrm(ks[9], (D_MODEL,), 0.02)
    peer_w_query = nrm(ks[10], (D_MODEL, PEER_HEADS * PEER_QUERY_DIM), D_MODEL ** -0.5)
    peer_sub_keys = nrm(ks[11], (PEER_HEADS, 2, PEER_N_KEYS, PEER_QUERY_DIM // 2), (PEER_QUERY_DIM // 2) ** -0.5)
    peer_u = nrm(ks[12], (PEER_N_EXPERTS, D_MODEL), D_MODEL ** -0.5)
    peer_v = nrm(ks[13], (PEER_N_EXPERTS, D_MODEL), DEEPNORM_BETA)
    ln2_g = 1.0 + nrm(ks[14], (D_MODEL,), 0.02)
    ln2_b = nrm(ks[15], (D_MODEL,), 0.02)
    return {'x': x, 'positions': positions, 'w_in': w_in, 'attn_sinks': attn_sinks,
            'conv_w': conv_w, 'a_log': a_log, 'dt_bias': dt_bias, 'dn_norm_g': dn_norm_g,
            'w_out': w_out, 'ln1_g': ln1_g, 'ln1_b': ln1_b, 'peer_w_query': peer_w_query,
            'peer_sub_keys': peer_sub_keys, 'peer_u': peer_u, 'peer_v': peer_v,
            'ln2_g': ln2_g, 'ln2_b': ln2_b}

def reference(x, positions, w_in, attn_sinks, conv_w, a_log, dt_bias, dn_norm_g, w_out,
              ln1_g, ln1_b, peer_w_query, peer_sub_keys, peer_u, peer_v, ln2_g, ln2_b):
    h = x
    for _ in range(DEPTH):
        mix = hybrid_mixer(h, positions, w_in, attn_sinks, conv_w, a_log, dt_bias, dn_norm_g, w_out)
        h = layer_norm(DEEPNORM_ALPHA * h + mix, ln1_g, ln1_b)
        ffn = peer_ffn(h, peer_w_query, peer_sub_keys, peer_u, peer_v)
        h = layer_norm(DEEPNORM_ALPHA * h + ffn, ln2_g, ln2_b)
    return h


_drawn_inputs = setup_inputs


def setup_inputs(seed=0):
    import zlib

    import numpy as np

    out = dict(_drawn_inputs(seed))
    spreads = {}
    factors = {'attn_sinks': 8.0, 'dn_norm_g': 3.142, 'ln2_g': 2.875, 'ln2_b': 2.865}
    for name, (base, spread) in spreads.items():
        noise = np.random.default_rng([zlib.crc32(name.encode()), seed]).standard_normal(out[name].shape)
        drawn = base * np.exp(spread * noise) if base else spread * noise
        out[name] = __import__('jax').numpy.asarray(drawn.astype(out[name].dtype))
    for name, factor in factors.items():
        out[name] = (out[name] * factor).astype(out[name].dtype)
    return out
```

```python
import math
from contextlib import ExitStack

import numpy as np

import concourse.bass as bass
from concourse import mybir
from concourse.alu_op_type import AluOpType as ALU

ACT = mybir.ActivationFunctionType
AX = mybir.AxisListType
F32, I32, U32 = mybir.dt.float32, mybir.dt.int32, mybir.dt.uint32

P = 128
SEQ, D = 1024, 1024
NB = SEQ // P
KT = D // P
HEADS, KV, HD = 8, 2, 64
GROUP = HEADS // KV
HALF = HD // 2
DH, DK = 4, 128
CHUNK = 64
TAPS = 4
PH, KEYS, TOPK = 8, 128, 16
LISTS = 2 * PH
SLOTS = PH * TOPK
ALPHA = 2.0 ** 0.25
LN_EPS, RMS_EPS, L2_EPS = 1e-5, 1e-6, 1e-6
NEG = -1e30
LOWEST = -3e38
W = 256
IN_CHUNKS = (HEADS * HD + 2 * KV * HD + 4 * DH * DK) // W
OUT_CHUNKS = D // W
Q_CHUNKS = LISTS * P // W
CHUNKS = IN_CHUNKS + OUT_CHUNKS + Q_CHUNKS
RING = 8
GROUPED = 4
DIAGS = 4
TWO_PI = (6.28125, 2029.0 / 2 ** 20, 2 * math.pi - 6.28125 - 2029.0 / 2 ** 20)

CONSTS = {}
_at = 0
for _name, _width in (("ident", P), ("ones", P), ("upto", P), ("strict", P), ("same16", P), ("off32", P),
                      ("off64", P), ("same64", P), ("band", 2 * P), ("iota", TOPK),
                      ("freq", HALF), ("eps_ln", 1), ("eps_rms", 1), ("eps_l2", 1), ("ln_qscale", 1)):
    CONSTS[_name] = (_at, _at + _width)
    _at += _width
CONST_COLS = _at


def constants():
    i, j = np.arange(P)[:, None], np.arange(P)[None, :]
    same = lambda w: (i // w) == (j // w)
    c = np.arange(2 * P)[None, :]
    full = lambda v: np.full((P, 1), v)
    row = lambda v: np.broadcast_to(np.asarray(v)[None, :], (P, len(v)))
    parts = {
        "ident": i == j, "ones": np.ones((P, P)),
        "upto": (i <= j) & same(CHUNK),
        "strict": (i > j) & same(CHUNK),
        "same16": same(16), "off32": same(32) & ~same(16), "off64": same(64) & ~same(32),
        "same64": same(CHUNK),
        "band": np.where((c > i) & (c <= i + P), 0.0, NEG),
        "iota": row(np.arange(TOPK)),
        "freq": row(np.float32(10000.0) ** (-np.arange(HALF, dtype=np.float32) / np.float32(HALF))),
        "eps_ln": full(LN_EPS), "eps_rms": full(RMS_EPS), "eps_l2": full(L2_EPS),
        "ln_qscale": full(math.log(DK ** -0.5)),
    }
    return np.concatenate([np.asarray(parts[k], np.float32) for k in CONSTS], axis=1)


class Signal:

    def __init__(self, sem, per_block, before):
        self.sem, self.per_block, self.before = sem, per_block, before

    def at(self, n, k):
        assert k + self.before > 0
        return self.sem, n * self.per_block + (k + self.before)


def build(nc, io):
    ctx = ExitStack()
    with ctx:
        def sb(name, cols, dt=F32, parts=P):
            return ctx.enter_context(nc.sbuf_tensor(name, [parts, cols], dt))

        def sem(name):
            return ctx.enter_context(nc.semaphore(name))

        def signal(name, per_block=1, before=0):
            return Signal(sem(name), per_block, before)

        bank = [ctx.enter_context(nc.psum_tensor(f"bank{i}", [P, 512], F32)) for i in range(6)]
        expert_sum = [ctx.enter_context(nc.psum_tensor(f"expert_sum{i}", [P, 512], F32)) for i in range(2)]

        const = sb("const", CONST_COLS)
        C = {k: const[:, a:b] for k, (a, b) in CONSTS.items()}
        ln1g, ln1b, ln2g, ln2b = (sb(x, D) for x in ("ln1g_sb", "ln1b_sb", "ln2g_sb", "ln2b_sb"))
        w_ba = sb("w_ba", KT * 2 * DH)
        sub_keys = sb("sub_keys", LISTS * KEYS)
        conv_w = sb("conv_w", 3 * DH * TAPS)
        neg_a = sb("neg_a", DH)
        dt_b = sb("dt_b", DH)
        norm_g = sb("norm_g", DK)
        sinks = sb("sinks", HEADS)
        cos = sb("cos", NB * HALF)
        sin = sb("sin", NB * HALF)
        mask = sb("mask", 2 * P)

        state = sb("state", DH * DK)
        k_keys = sb("k_keys", KV * 2 * P, parts=HD)
        v_rows = sb("v_rows", 2 * KV * HD)
        conv_in = sb("conv_in", 3 * DH * (P + TAPS - 1))

        chunk = [sb(f"chunk{i}", KT * W) for i in range(2)]
        ring = sb("ring", RING * 2 * D)
        xT = sb("xT", KT * P)
        x_in = sb("x_in", D)

        conv = sb("conv", 3 * DH * P)
        z = sb("z", DH * DK)
        o_cat = sb("o_cat", D)
        oT = sb("oT", KT * P)
        x1 = sb("x1", D)
        small = sb("small", 256)
        tiles = 25
        arena = sb("arena", tiles * 512)
        expert = sb("expert", SLOTS, U32)
        gate = sb("gate", SLOTS)
        h_raw = sb("h_raw", SLOTS)
        h_w = sb("h_w", SLOTS)
        diag = sb("diag", DIAGS * P)

        def tile(i, k=1):
            return arena[:, i * 512:(i + k) * 512]

        def by_head(ap, h=DH):
            return ap.rearrange("p (h c) -> p h c", h=h)

        def col(i, k=1):
            return small[:, i:i + k]

        def over_cols(ap, k):
            return ap.unsqueeze(2).to_broadcast([P, ap.shape[1], k])

        def over_heads(ap, h):
            return ap.unsqueeze(1).to_broadcast([P, h, ap.shape[1]])

        S_BETA, S_EB, S_AX, S_NX, S_MN, S_SP, S_G, S_GC, S_GL, S_EGC, S_BG, S_KD = (4 * i for i in range(12))
        S_MAX, S_NMAX, S_SUM, S_SNK, S_DEN, S_RIN = (48 + 8 * i for i in range(6))
        S_SS, S_VE, S_LN, S_R, S_T = (96 + 4 * i for i in range(5))
        S_BN, S_MV, S_RS = 120, 132, 136
        S_GM, S_GS, S_GR = 160, 168, 176
        S_RT = 184

        setup_in = sem("setup_in")
        passed = sem("passed")
        setup_steps = sem("setup_steps")
        angles = sem("angles")
        tables = sem("tables")
        neg_a_ready = sem("neg_a_ready")

        xT_in = signal("xT_in", 16)
        x_loaded = signal("x_loaded", 16)
        chunk_in = [signal(f"chunk_in{i}", 16 * ((CHUNKS + 1 - i) // 2)) for i in range(2)]
        chunk_used = signal("chunk_used", CHUNKS, before=1)
        att_copied = signal("att_copied", 2)
        conv_copied = signal("conv_copied", 3)
        z_copied = signal("z_copied", 1)
        roped = signal("roped", 2)
        att_T = signal("att_T", 2)
        att_Tc = signal("att_Tc", 3)
        scored = signal("scored", 4)
        masked = signal("masked", 4)
        neg_max = signal("neg_max", 1)
        probs = signal("probs", 9)
        probs_T = signal("probs_T", 4)
        probs_Tc = signal("probs_Tc", 4)
        att_o = signal("att_o", 1)
        att_kept = signal("att_kept", 1, before=1)
        att_out = signal("att_out", 1)
        tap0 = signal("tap0", 3 * DH)
        conv_step = signal("conv_step", 3 * DH * (TAPS - 1))
        conv_tail = signal("conv_tail", 1, before=1)
        silu_done = signal("silu_done", 2)
        squares = signal("squares", 1)
        norms = signal("norms", 2)
        inv_norms = signal("inv_norms", 1)
        qk_normed = signal("qk_normed", 1)
        gate_pre = signal("gate_pre", 1)
        gate_exp = signal("gate_exp", 2)
        g_ready = signal("g_ready", 2)
        g_sums = signal("g_sums", 2)
        gc_copied = signal("gc_copied", 2)
        kd_pre = signal("kd_pre", 1)
        kd_exp = signal("kd_exp", 1)
        diffs = signal("diffs", 2)
        decays = signal("decays", 2)
        ktok = signal("ktok", 4)
        a_ready = signal("a_ready", 1)
        aT = signal("aT", 1)
        nT_ready = signal("nT_ready", 1)
        x0_ready = signal("x0_ready", 1)
        sq = signal("sq", 5)
        sq_copied = signal("sq_copied", 5)
        prod = signal("prod", 3)
        prod_added = signal("prod_added", 3)
        turn = signal("turn", 4)
        turn_copied = signal("turn_copied", 4)
        merge = signal("merge", 2)
        merged = signal("merged", 2)
        scaled = signal("scaled", 5)
        solved = signal("solved", 2)
        solved_copied = signal("solved_copied", 2)
        w_state = signal("w_state", 2)
        v_new = signal("v_new", 2)
        o_done = signal("o_done", 2)
        kv_done = signal("kv_done", 2)
        state_new = signal("state_new", 2, before=1)
        o_copied = signal("o_copied", 2)
        o_squares = signal("o_squares", 1)
        o_ms = signal("o_ms", 1)
        root = signal("root", 3)
        dn_out = signal("dn_out", 1)
        o_T = signal("o_T", 2)
        o_Tc = signal("o_Tc", 2)
        residual = signal("residual", 1, before=1)
        var_ready = signal("var_ready", 2)
        x1_ready = signal("x1_ready", 1)
        x1_T = signal("x1_T", 2)
        x1_Tc = signal("x1_Tc", 2)
        queries_c = signal("queries_c", 4)
        key_scores = signal("key_scores", 4)
        key_scores_c = signal("key_scores_c", 4, before=1)
        best_sub = signal("best_sub", 1)
        best_exp = signal("best_exp", 1)
        chosen = signal("chosen", 2)
        gathered = [signal(f"gathered{i}", 16 * SLOTS // RING) for i in range(RING)]
        dotted = signal("dotted", SLOTS)
        gelued = signal("gelued", SLOTS // GROUPED)
        weighted = signal("weighted", SLOTS // GROUPED)
        diag_ready = signal("diag_ready", SLOTS)
        added = signal("added", SLOTS, before=1)
        out_ready = signal("out_ready", 1, before=1)
        stored = signal("stored", 16, before=16)
        DVE_STEPS, ACT_STEPS = 131, 7
        dve_done = signal("dve_done", DVE_STEPS)
        act_done = signal("act_done", ACT_STEPS)

        conv3 = conv_in[:, :].rearrange("p (t c) -> p t c", t=3 * DH)
        convo = conv[:, :].rearrange("p (t c) -> p t c", t=3 * DH)
        keysT = k_keys[:, :].rearrange("p (g c) -> p g c", g=KV)
        vrows = v_rows[:, :].rearrange("p (s c) -> p s c", s=2)
        ring3 = ring[:, :].rearrange("p (r c) -> p r c", r=RING)

        A_ROT, A_T = 16, 18
        A_QT = 21
        A_P, A_PT = 0, 4
        A_ATT = 14
        att = arena[:, A_ATT * 512:(A_ATT + 2) * 512]
        A_SQ = 23
        (A_UG, A_EG, A_DD, A_DI, A_DT, A_A, A_NT, A_E32, A_E64, A_R, A_N2, A_N2T, A_N4, A_N4T, A_N8,
         A_Z, A_TT, A_KBG, A_KDEC, A_VB, A_QKT, A_QDT, A_U, A_WT, A_VN) = range(25)
        A_N, A_O = A_UG, A_DD
        A_QP, A_S, A_CAND, A_HOT, A_BEST = 0, 4, 8, 12, 16
        best = [arena[:, (A_BEST * 512 + i * LISTS * TOPK):(A_BEST * 512 + (i + 1) * LISTS * TOPK)] for i in range(3)]
        best_v, best_i, best_if = best[0], best[1].bitcast(U32), best[2]
        top = [arena[:, (A_BEST + 2) * 512 + i * SLOTS:(A_BEST + 2) * 512 + (i + 1) * SLOTS] for i in range(5)]
        top_v, top_p, pos_hi, pos_lo, pos_u = top[0], top[1].bitcast(U32), top[2], top[3], top[4].bitcast(U32)

        rot = arena[:, A_ROT * 512:A_ROT * 512 + 640].rearrange("p (h c) -> p h c", c=HD)
        rtmp = [arena[:, A_T * 512 + 320 * i:A_T * 512 + 320 * (i + 1)].rearrange("p (h c) -> p h c", c=HALF)
                for i in range(4)]

        positions_in = arena[:, 0:NB].bitcast(I32)
        block = ctx.enter_context(nc.Block())
        setup = 16 * 13

        def alone(eng):
            eng.sem_inc(passed, 1)

        @block.sync
        def _(sp):
            sp.sem_inc(stored.sem, 16)
            for dst, src in ((const, io["consts"]), (w_ba, io["w_ba"]), (sub_keys, io["sub_keys"]),
                             (conv_w, io["conv_w"])):
                sp.dma_start(dst[:, :], src).then_inc(setup_in, 16)
            sp.dma_start(positions_in, io["positions"]).then_inc(setup_in, 16)
            for dst, src in ((ln1g, "ln1_g"), (ln1b, "ln1_b"), (ln2g, "ln2_g"), (ln2b, "ln2_b"), (neg_a, "a_log"),
                             (dt_b, "dt_bias"), (norm_g, "dn_norm_g"), (sinks, "attn_sinks")):
                sp.dma_start(dst[:, :], io[src].partition_broadcast(P)).then_inc(setup_in, 16)
            with sp.Fori(0, NB) as n:
                sp.wait_ge(*chunk_used.at(n, 0))
                alone(sp)
                sp.dma_start(xT[:, :], io["xT"][bass.ds(n, 1), :, :].rearrange("n p c -> (n p) c")).then_inc(xT_in.sem, 16)
                sp.wait_ge(*residual.at(n, 0))
                alone(sp)
                sp.dma_start(x_in[:, :], io["x"][bass.ds(n, 1), :, :].rearrange("n p c -> (n p) c")).then_inc(x_loaded.sem, 16)
                for c in range(CHUNKS):
                    sp.wait_ge(*chunk_used.at(n, max(c - 1, 0)))
                    alone(sp)
                    sp.dma_start(chunk[c % 2][:, :], io["weights"][c]).then_inc(chunk_in[c % 2].sem, 16)
            sp.wait_ge(*stored.at(NB, 0))

        @block.gpsimd
        def _(pool):
            with pool.Fori(0, NB) as n:
                pool.wait_ge(*chosen.at(n, 1))
                for j in range(SLOTS):
                    pool.wait_ge(*added.at(n, max(j - RING + 1, 0)))
                    alone(pool)
                    pool.indirect_dma_start(
                        out=ring[:, (j % RING) * 2 * D:(j % RING + 1) * 2 * D], out_offset=None, in_=io["uv"],
                        in_offset=bass.IndirectOffsetOnAxis(ap=expert[:, j:j + 1], axis=0),
                    ).then_inc(gathered[j % RING].sem, 16)

        @block.tensor
        def _(pe):
            ident = C["ident"]
            xTv = xT[:, :].rearrange("p (k c) -> p k c", k=KT)
            oTv = oT[:, :].rearrange("p (k c) -> p k c", k=KT)
            ch = [c[:, :].rearrange("p (k c) -> p k c", k=KT) for c in chunk]
            ba = w_ba[:, :].rearrange("p (k c) -> p k c", k=KT)
            sk = sub_keys[:, :].rearrange("p (l c) -> p l c", l=LISTS)

            def use_chunk(n, c):
                pe.wait_ge(*chunk_in[c % 2].at(n, 16 * (c // 2 + 1)))
                return ch[c % 2]

            def tokens_out(n, c, out, act):
                w = use_chunk(n, c)
                for k in range(KT):
                    mm = pe.matmul(out, act[:, k, :], w[:, k, :], start=(k == 0), stop=(k == KT - 1))
                mm.then_inc(chunk_used.sem, 1)

            def channels_out(n, c, outs, act):
                w = use_chunk(n, c)
                for i, out in enumerate(outs):
                    for k in range(KT):
                        mm = pe.matmul(out, w[:, k, i * P:(i + 1) * P], act[:, k, :], start=(k == 0), stop=(k == KT - 1))
                mm.then_inc(chunk_used.sem, 1)

            def each_head(out, lhsT, rhs):
                for h in range(DH):
                    hs = slice(h * P, (h + 1) * P)
                    mm = pe.matmul(out[:, hs], lhsT[:, hs], rhs[:, hs], start=True, stop=True)
                return mm

            def turn_each(out, in_, k=4, parts=P):
                for h in range(k):
                    mm = pe.transpose(out[:, h * P:(h + 1) * P], in_[:, h * P:(h + 1) * P], ident)
                return mm

            pe.wait_ge(setup_in, setup)
            pe.sem_inc(chunk_used.sem, 1)
            pe.sem_inc(added.sem, 1)
            with pe.Fori(0, NB) as n:
                pe.wait_ge(*xT_in.at(n, 16))
                pe.wait_ge(*key_scores_c.at(n, 0))
                tokens_out(n, 0, bank[0][:, 0:W], xTv)
                tokens_out(n, 1, bank[0][:, W:2 * W], xTv)
                for k in range(KT):
                    pe.matmul(bank[1][:, W:W + 2 * DH], xTv[:, k, :], ba[:, k, :], start=(k == 0), stop=(k == KT - 1))
                tokens_out(n, 2, bank[1][:, 0:W], xTv)
                for t in range(3):
                    for i in range(2):
                        channels_out(n, 3 + 2 * t + i, [bank[3 + t][:, (2 * i + j) * P:(2 * i + j + 1) * P] for j in range(2)], xTv)
                tokens_out(n, 9, bank[2][:, 0:W], xTv)
                tokens_out(n, 10, bank[2][:, W:2 * W], xTv)

                pe.wait_ge(*roped.at(n, 2))
                pe.wait_ge(*att_copied.at(n, 2))
                alone(pe)
                for h in range(HEADS):
                    mm = pe.transpose(bank[h // 4][0:HD, (h % 4) * P:(h % 4 + 1) * P], rot[:, h, :], ident)
                mm.then_inc(att_T.sem, 1)
                pe.wait_ge(*z_copied.at(n, 1))
                alone(pe)
                for g in range(KV):
                    mm = pe.transpose(bank[2][0:HD, g * P:(g + 1) * P], rot[:, HEADS + g, :], ident)
                mm.then_inc(att_T.sem, 1)
                pe.wait_ge(*att_Tc.at(n, 3))
                pe.wait_ge(*conv_copied.at(n, 3))
                for h in range(HEADS):
                    mm = pe.matmul(bank[2 + h // 2][:, (h % 2) * 2 * P:(h % 2 + 1) * 2 * P],
                                   arena[0:HD, A_QT * 512 + h * P:A_QT * 512 + (h + 1) * P], keysT[:, h // GROUP, :],
                                   start=True, stop=True)
                    if h % 2:
                        mm.then_inc(scored.sem, 1)
                pe.wait_ge(*masked.at(n, 4))
                for h in range(HEADS):
                    pe.wait_ge(*probs.at(n, h + 1))
                    for s in range(2):
                        i = 2 * h + s
                        mm = pe.transpose(bank[i // 4][:, (i % 4) * P:(i % 4 + 1) * P],
                                          arena[:, A_P * 512 + i * P:A_P * 512 + (i + 1) * P], ident)
                    if h % 2:
                        mm.then_inc(probs_T.sem, 1)
                for h in range(HEADS):
                    if h % 2 == 0:
                        pe.wait_ge(*probs_Tc.at(n, h // 2 + 1))
                    g = h // GROUP
                    for s in range(2):
                        i = 2 * h + s
                        mm = pe.matmul(bank[4][:, h * HD:(h + 1) * HD], arena[:, A_PT * 512 + i * P:A_PT * 512 + (i + 1) * P],
                                       vrows[:, s, g * HD:(g + 1) * HD], start=(s == 0), stop=(s == 1))
                mm.then_inc(att_o.sem, 1)

                pe.wait_ge(*squares.at(n, 1))
                for i in range(2):
                    pe.matmul(bank[2 + i][:, :], C["ones"], tile(A_SQ + i), start=True, stop=True).then_inc(norms.sem, 1)
                pe.wait_ge(*g_ready.at(n, 2))
                pe.matmul(bank[1][:, 0:DH], C["upto"], col(S_G, DH), start=True, stop=True)
                pe.matmul(bank[1][:, DH:2 * DH], C["same64"], col(S_G, DH), start=True, stop=True).then_inc(g_sums.sem, 1)
                pe.matmul(bank[0][:, :], C["ones"], tile(A_UG), start=True, stop=True).then_inc(g_sums.sem, 1)
                pe.wait_ge(*qk_normed.at(n, 1))
                qn, kn, vn = (conv[:, i * 512:(i + 1) * 512] for i in range(3))
                pe.wait_ge(*inv_norms.at(n, 1))
                turn_each(bank[3], kn).then_inc(ktok.sem, 1)
                each_head(bank[5], kn, kn).then_inc(ktok.sem, 1)
                pe.wait_ge(*att_out.at(n, 1))
                turn_each(bank[4], vn).then_inc(ktok.sem, 1)
                each_head(bank[2], kn, qn).then_inc(ktok.sem, 1)
                pe.wait_ge(*a_ready.at(n, 1))
                pe.wait_ge(*decays.at(n, 2))
                turn_each(bank[0], tile(A_A)).then_inc(aT.sem, 1)
                pe.wait_ge(*nT_ready.at(n, 1))
                each_head(bank[1], tile(A_NT), tile(A_N)).then_inc(sq.sem, 1)
                pe.wait_ge(*scaled.at(n, 2))
                each_head(bank[3], tile(A_N), tile(A_NT)).then_inc(sq.sem, 1)
                pe.wait_ge(*sq_copied.at(n, 2))
                pe.wait_ge(*scaled.at(n, 3))
                each_head(bank[4], tile(A_N2T), tile(A_N2)).then_inc(sq.sem, 1)
                each_head(bank[5], tile(A_N2), tile(A_N2T)).then_inc(sq.sem, 1)
                pe.wait_ge(*x0_ready.at(n, 1))
                each_head(bank[0], tile(A_N2), tile(A_R)).then_inc(prod.sem, 1)
                pe.wait_ge(*sq_copied.at(n, 4))
                each_head(bank[1], tile(A_N4T), tile(A_N4)).then_inc(sq.sem, 1)
                pe.wait_ge(*prod_added.at(n, 1))
                each_head(bank[3], tile(A_N4), tile(A_R)).then_inc(prod.sem, 1)
                pe.wait_ge(*sq_copied.at(n, 5))
                pe.wait_ge(*prod_added.at(n, 2))
                each_head(bank[4], tile(A_N8), tile(A_R)).then_inc(prod.sem, 1)
                for m, (e, b) in enumerate(((A_E32, (5, 0, 1)), (A_E64, (3, 4, 5)))):
                    if m == 0:
                        pe.wait_ge(*prod_added.at(n, 3))
                    else:
                        pe.wait_ge(*merged.at(n, 1))
                    each_head(bank[b[0]], tile(e), tile(A_R)).then_inc(turn.sem, 1)
                    turn_each(bank[b[1]], tile(A_R)).then_inc(turn.sem, 1)
                    pe.wait_ge(*turn_copied.at(n, 2 * m + 2))
                    each_head(bank[b[2]], tile(A_TT), tile(A_Z)).then_inc(merge.sem, 1)
                pe.wait_ge(*merged.at(n, 2))
                each_head(bank[0], tile(A_R), tile(A_VB)).then_inc(solved.sem, 1)
                each_head(bank[1], tile(A_KBG), tile(A_R)).then_inc(solved.sem, 1)
                pe.wait_ge(*solved_copied.at(n, 2))
                pe.wait_ge(*scaled.at(n, 5))
                for c, (bw, bo, bk) in enumerate(((3, 2, 4), (5, 0, 1))):
                    rows = slice(c * CHUNK, (c + 1) * CHUNK)
                    if c == 0:
                        pe.wait_ge(*state_new.at(n, 0))
                    else:
                        pe.wait_ge(*state_new.at(n, 1))
                    each_head(bank[bw], tile(A_WT), state[:, :]).then_inc(w_state.sem, 1)
                    pe.wait_ge(*v_new.at(n, c + 1))
                    for h in range(DH):
                        hs = slice(h * P, (h + 1) * P)
                        mm = pe.matmul(bank[bk][:, hs], tile(A_KDEC)[rows, hs], tile(A_VN)[rows, hs], start=True, stop=True)
                    mm.then_inc(kv_done.sem, 1)
                    for h in range(DH):
                        hs = slice(h * P, (h + 1) * P)
                        pe.matmul(bank[bo][:, hs], tile(A_QDT)[:, hs], state[:, hs], start=True, stop=False)
                        mm = pe.matmul(bank[bo][:, hs], tile(A_QKT)[rows, hs], tile(A_VN)[rows, hs], start=False, stop=True)
                    mm.then_inc(o_done.sem, 1)

                pe.wait_ge(*dn_out.at(n, 1))
                for i in range(2):
                    turn_each(bank[1 + i], o_cat[:, i * 512:(i + 1) * 512]).then_inc(o_T.sem, 1)
                pe.wait_ge(*o_Tc.at(n, 2))
                for c in range(OUT_CHUNKS):
                    tokens_out(n, IN_CHUNKS + c, bank[3 + c // 2][:, (c % 2) * W:(c % 2 + 1) * W], oTv)

                pe.wait_ge(*x1_ready.at(n, 1))
                for i, b in enumerate((5, 0)):
                    turn_each(bank[b], x1[:, i * 512:(i + 1) * 512]).then_inc(x1_T.sem, 1)
                pe.wait_ge(*x1_Tc.at(n, 2))
                for c in range(Q_CHUNKS):
                    b = bank[1 + c // 2]
                    channels_out(n, IN_CHUNKS + OUT_CHUNKS + c, [b[:, (2 * (c % 2) + j) * P:(2 * (c % 2) + j + 1) * P] for j in range(2)], oTv)
                for i, b in enumerate((5, 0, 1, 2)):
                    pe.wait_ge(*queries_c.at(n, min(i + 1, 4)))
                    if i == 2:
                        pe.wait_ge(*queries_c.at(n, 4))
                    for j in range(4):
                        l = 4 * i + j
                        mm = pe.matmul(bank[b][:, j * P:(j + 1) * P], arena[:, A_QP * 512 + l * P:A_QP * 512 + (l + 1) * P],
                                       sk[:, l, :], start=True, stop=True)
                    mm.then_inc(key_scores.sem, 1)

                pe.wait_ge(*out_ready.at(n, 0))
                for j in range(SLOTS):
                    pe.wait_ge(*gathered[j % RING].at(n, 16 * (j // RING + 1)))
                    pe.wait_ge(*diag_ready.at(n, j + 1))
                    for i in range(2):
                        mm = pe.matmul(expert_sum[i][:, :], diag[:, (j % DIAGS) * P:(j % DIAGS + 1) * P],
                                       ring3[:, j % RING, D + i * 512:D + (i + 1) * 512],
                                       start=(j == 0), stop=(j == SLOTS - 1))
                    mm.then_inc(added.sem, 1)

        @block.scalar
        def _(act):
            steps = [0]

            def then(n, ins):
                steps[0] += 1
                ins.then_inc(act_done.sem, 1)
                act.wait_ge(*act_done.at(n, steps[0]))

            def rsqrt_start(n, out, in_, eps):
                then(n, act.activation(out, in_, ACT.Ln, bias=eps))
                act.activation(out, out, ACT.Exp, scale=-0.5).then_inc(root.sem, 1)

            act.wait_ge(setup_in, setup)
            act.sem_inc(key_scores_c.sem, 1)
            act.activation(neg_a[:, :], neg_a[:, :], ACT.Exp).then_inc(neg_a_ready, 1)
            act.wait_ge(angles, 1)
            act.activation(sin[:, :], sin[:, :], ACT.Sin).then_inc(tables, 1)
            act.activation(cos[:, :], cos[:, :], ACT.Sin).then_inc(tables, 1)

            with act.Fori(0, NB) as n:
                act.wait_ge(*chunk_used.at(n, 2))
                act.copy(att[:, 0:512], bank[0][:, :]).then_inc(att_copied.sem, 1)
                act.wait_ge(*chunk_used.at(n, 3))
                act.copy(att[:, 512:776], bank[1][:, 0:264]).then_inc(att_copied.sem, 1)
                act.wait_ge(*conv_tail.at(n, 0))
                for t in range(3):
                    act.wait_ge(*chunk_used.at(n, 5 + 2 * t))
                    act.copy(conv3[:, DH * t:DH * (t + 1), TAPS - 1:TAPS - 1 + P], by_head(bank[3 + t][:, :])).then_inc(conv_copied.sem, 1)
                act.wait_ge(*chunk_used.at(n, IN_CHUNKS))
                act.copy(z[:, :], bank[2][:, :]).then_inc(z_copied.sem, 1)
                act.wait_ge(*gate_pre.at(n, 1))
                act.activation(col(S_EB, DH), att[:, 768:772], ACT.Exp, scale=-1.0)
                then(n, act.activation(col(S_SP, DH), col(S_MN, DH), ACT.Exp))
                act.activation(col(S_SP, DH), col(S_SP, DH), ACT.Ln, bias=1.0).then_inc(gate_exp.sem, 2)
                act.wait_ge(*att_T.at(n, 1))
                for i in range(2):
                    act.copy(arena[0:HD, (A_QT + i) * 512:(A_QT + i + 1) * 512], bank[i][0:HD, :]).then_inc(att_Tc.sem, 1)
                act.wait_ge(*att_T.at(n, 2))
                act.wait_ge(*att_kept.at(n, 0))
                act.copy(keysT[:, :, P:2 * P], by_head(bank[2][0:HD, 0:2 * P], KV)).then_inc(att_Tc.sem, 1)
                act.wait_ge(*conv_copied.at(n, 3))
                for t in range(3 * DH):
                    act.activation(convo[:, t, :], conv3[:, t, 0:P], ACT.Copy, scale=conv_w[:, t * TAPS:t * TAPS + 1]).then_inc(tap0.sem, 1)
                act.wait_ge(*neg_max.at(n, 1))
                for h in range(HEADS):
                    pr = arena[:, A_P * 512 + h * 2 * P:A_P * 512 + (h + 1) * 2 * P]
                    act.activation(pr, pr, ACT.Exp, bias=col(S_NMAX + h), accum_out=col(S_SUM + h)).then_inc(probs.sem, 1)
                act.activation(col(S_SNK, HEADS), col(S_SNK, HEADS), ACT.Exp).then_inc(probs.sem, 1)
                for i in range(4):
                    act.wait_ge(*probs_T.at(n, i + 1))
                    act.copy(tile(A_PT + i), bank[i][:, :]).then_inc(probs_Tc.sem, 1)
                act.wait_ge(*conv_step.at(n, 3 * DH * (TAPS - 1)))
                then(n, act.activation(conv[:, :], conv[:, :], ACT.Silu))
                act.activation(z[:, :], z[:, :], ACT.Silu).then_inc(silu_done.sem, 2)
                act.activation(tile(A_SQ, 2), conv[:, 0:2 * 512], ACT.Square).then_inc(squares.sem, 1)
                act.wait_ge(*att_o.at(n, 1))
                act.copy(keysT[:, :, 0:P], keysT[:, :, P:2 * P])
                act.copy(vrows[:, 0, :], vrows[:, 1, :]).then_inc(att_kept.sem, 1)
                act.wait_ge(*norms.at(n, 2))
                for i in range(2):
                    ins = act.activation(tile(A_SQ + i), bank[2 + i][:, :], ACT.Ln, bias=C["eps_l2"])
                then(n, ins)
                act.activation(tile(A_SQ), tile(A_SQ), ACT.Exp, scale=-0.5, bias=C["ln_qscale"])
                act.activation(tile(A_SQ + 1), tile(A_SQ + 1), ACT.Exp, scale=-0.5).then_inc(inv_norms.sem, 1)
                act.wait_ge(*g_sums.at(n, 2))
                then(n, act.copy(col(S_GC, 2 * DH), bank[1][:, 0:2 * DH]))
                act.activation(col(S_EGC, DH), col(S_GC, DH), ACT.Exp).then_inc(gc_copied.sem, 1)
                act.activation(tile(A_EG), bank[0][:, :], ACT.Exp).then_inc(gc_copied.sem, 1)
                act.wait_ge(*kd_pre.at(n, 1))
                act.activation(col(S_KD, DH), col(S_KD, DH), ACT.Exp).then_inc(kd_exp.sem, 1)
                act.wait_ge(*diffs.at(n, 1))
                act.activation(tile(A_DI), tile(A_DI), ACT.Exp, scale=-1.0).then_inc(decays.sem, 1)
                act.wait_ge(*diffs.at(n, 2))
                act.activation(tile(A_DT), tile(A_DT), ACT.Exp).then_inc(decays.sem, 1)
                for k, (dst, b) in enumerate(((A_N2, 1), (A_N2T, 3), (A_N4, 4), (A_N4T, 5), (A_N8, 1))):
                    act.wait_ge(*sq.at(n, k + 1))
                    act.copy(tile(dst), bank[b][:, :]).then_inc(sq_copied.sem, 1)
                for k, (dst, b) in enumerate(((A_Z, 5), (A_TT, 0), (A_Z, 3), (A_TT, 4))):
                    act.wait_ge(*turn.at(n, k + 1))
                    act.copy(tile(dst), bank[b][:, :]).then_inc(turn_copied.sem, 1)
                for k, (dst, b) in enumerate(((A_U, 0), (A_WT, 1))):
                    act.wait_ge(*solved.at(n, k + 1))
                    act.copy(tile(dst), bank[b][:, :]).then_inc(solved_copied.sem, 1)
                for c, b in enumerate((2, 0)):
                    rows = slice(c * CHUNK, (c + 1) * CHUNK)
                    act.wait_ge(*o_done.at(n, c + 1))
                    act.copy(tile(A_O)[rows, :], bank[b][rows, :]).then_inc(o_copied.sem, 1)
                act.wait_ge(*o_ms.at(n, 1))
                rsqrt_start(n, col(S_RT, DH), col(S_SS, DH), C["eps_rms"])
                for i in range(2):
                    act.wait_ge(*o_T.at(n, i + 1))
                    act.copy(oT[:, i * 512:(i + 1) * 512], bank[1 + i][:, :]).then_inc(o_Tc.sem, 1)
                act.wait_ge(*var_ready.at(n, 1))
                rsqrt_start(n, col(S_RT), col(S_MV + 1), C["eps_ln"])
                for i, b in enumerate((5, 0)):
                    act.wait_ge(*x1_T.at(n, i + 1))
                    act.copy(oT[:, i * 512:(i + 1) * 512], bank[b][:, :]).then_inc(x1_Tc.sem, 1)
                for i in range(4):
                    act.wait_ge(*chunk_used.at(n, IN_CHUNKS + OUT_CHUNKS + 2 * (i + 1)))
                    act.copy(tile(A_QP + i), bank[1 + i][:, :]).then_inc(queries_c.sem, 1)
                for i, b in enumerate((5, 0, 1, 2)):
                    act.wait_ge(*key_scores.at(n, i + 1))
                    act.copy(tile(A_S + i), bank[b][:, :]).then_inc(key_scores_c.sem, 1)
                act.wait_ge(*best_sub.at(n, 1))
                act.activation(gate[:, :], gate[:, :], ACT.Exp).then_inc(best_exp.sem, 1)
                for q in range(SLOTS // GROUPED):
                    s = slice(q * GROUPED, (q + 1) * GROUPED)
                    act.wait_ge(*dotted.at(n, (q + 1) * GROUPED))
                    act.activation(h_raw[:, s], h_raw[:, s], ACT.Gelu).then_inc(gelued.sem, 1)
                    act.wait_ge(*weighted.at(n, q + 1))
                    for j in range(q * GROUPED, (q + 1) * GROUPED):
                        act.wait_ge(*added.at(n, max(j - DIAGS + 1, 0)))
                        act.activation(diag[:, (j % DIAGS) * P:(j % DIAGS + 1) * P], C["ident"], ACT.Copy,
                                       scale=h_w[:, j:j + 1]).then_inc(diag_ready.sem, 1)
                act.wait_ge(*var_ready.at(n, 2))
                rsqrt_start(n, col(S_RT), col(S_MV + 1), C["eps_ln"])
                act.wait_ge(*out_ready.at(n, 1))
                act.dma_start(io["out"][bass.ds(n, 1), :, :].rearrange("n p c -> (n p) c"), o_cat[:, :]).then_inc(stored.sem, 16)
            assert steps[0] == ACT_STEPS, steps

        @block.vector
        def _(dve):
            steps = [0]
            setup_step = setup_steps

            def then(n, ins):
                steps[0] += 1
                ins.then_inc(dve_done.sem, 1)
                dve.wait_ge(*dve_done.at(n, steps[0]))

            count = [0]

            def first(ins):
                count[0] += 1
                ins.then_inc(setup_step, 1)
                dve.wait_ge(setup_step, count[0])

            tt, ts, stt = dve.tensor_tensor, dve.tensor_scalar, dve.scalar_tensor_tensor

            dve.memset(state[:, :], 0.0).then_inc(state_new.sem, 1)
            dve.memset(k_keys[:, :], 0.0)
            dve.memset(v_rows[:, :], 0.0).then_inc(att_kept.sem, 1)
            dve.memset(conv_in[:, :], 0.0).then_inc(conv_tail.sem, 1)
            for unused in (residual, out_ready):
                dve.sem_inc(unused.sem, 1)
            dve.wait_ge(setup_in, setup)
            first(dve.tensor_copy(mask[:, P:2 * P], C["band"][:, P:2 * P]))
            first(dve.memset(mask[:, 0:P], NEG))
            pos = small[:, 0:NB]
            c3 = lambda t: t[:, :].rearrange("p (n c) -> p n c", n=NB)
            turns_i = arena[:, 512:512 + NB * HALF].bitcast(I32)
            turns = arena[:, 1024:1024 + NB * HALF]
            over = arena[:, 1536:1536 + NB * HALF]
            first(dve.tensor_copy(pos, positions_in))
            first(tt(c3(sin), over_cols(pos, HALF), over_heads(C["freq"], NB), ALU.mult))
            first(ts(turns, sin[:, :], 1.0 / (2 * math.pi), None, ALU.mult))
            first(dve.tensor_copy(turns_i, turns))
            first(dve.tensor_copy(turns, turns_i))
            for part in TWO_PI:
                first(stt(out=sin[:, :], in0=turns, scalar=-part, in1=sin[:, :], op0=ALU.mult, op1=ALU.add))

            def wrap(t):
                for op, edge, shift in ((ALU.is_gt, math.pi, -2 * math.pi), (ALU.is_lt, -math.pi, 2 * math.pi)):
                    first(ts(over, t[:, :], edge, shift, op, ALU.mult))
                    first(tt(t[:, :], t[:, :], over, ALU.add))
            wrap(sin)
            first(ts(cos[:, :], sin[:, :], math.pi / 2, None, ALU.add))
            wrap(cos)
            first(ts(sin[:, :], sin[:, :], 3.1415925, -3.1415925, ALU.min, ALU.max))
            ts(cos[:, :], cos[:, :], 3.1415925, -3.1415925, ALU.min, ALU.max).then_inc(angles, 1)
            dve.wait_ge(neg_a_ready, 1)
            first(ts(neg_a[:, :], neg_a[:, :], -1.0, None, ALU.mult))
            dve.wait_ge(tables, 2)

            def refine(n, y, v, eps, t, k):
                then(n, tt(t, y, y, ALU.mult))
                then(n, stt(out=t, in0=v, scalar=eps, in1=t, op0=ALU.add, op1=ALU.mult))
                then(n, ts(t, t, -0.5, 1.5, ALU.mult, ALU.add))
                then(n, tt(y, y, t, ALU.mult))

            def layer_norm(n, x, g, b, out, which, last):
                bn = small[:, S_BN:S_BN + 12].rearrange("p (a c) -> p a c", a=2)
                for i in range(2):
                    ins = dve.bn_stats(bn[:, i, :], x[:, i * 512:(i + 1) * 512])
                then(n, ins)
                alone(dve)
                dve.bn_aggr(col(S_MV, 2), small[:, S_BN:S_BN + 12]).then_inc(var_ready.sem, 1)
                dve.wait_ge(*root.at(n, which))
                refine(n, col(S_RT), col(S_MV + 1), LN_EPS, col(S_RT + 1), 1)
                then(n, ts(x[:, :], x[:, :], col(S_MV), col(S_RT), ALU.subtract, ALU.mult))
                then(n, tt(x[:, :], x[:, :], g[:, :], ALU.mult))
                last(tt(out[:, :], x[:, :], b[:, :], ALU.add))

            with dve.Fori(0, NB) as n:
                dve.wait_ge(*att_copied.at(n, 2))
                then(n, tt(col(S_AX, DH), att[:, 772:776], dt_b[:, :], ALU.add))
                then(n, ts(col(S_NX, DH), col(S_AX, DH), -1.0, None, ALU.mult))
                tt(col(S_MN, DH), col(S_AX, DH), col(S_NX, DH), ALU.min).then_inc(gate_pre.sem, 1)
                qk = att[:, 0:640].rearrange("p (h c) -> p h c", c=HD)
                cs = cos[:, bass.ts(n, HALF)].unsqueeze(1).to_broadcast([P, HEADS + KV, HALF])
                sn = sin[:, bass.ts(n, HALF)].unsqueeze(1).to_broadcast([P, HEADS + KV, HALF])
                x_lo, x_hi = qk[:, :, 0:HALF], qk[:, :, HALF:HD]
                tt(rtmp[0], x_lo, cs, ALU.mult)
                tt(rtmp[1], x_hi, sn, ALU.mult)
                tt(rtmp[2], x_hi, cs, ALU.mult)
                then(n, tt(rtmp[3], x_lo, sn, ALU.mult))
                tt(rot[:, :, 0:HALF], rtmp[0], rtmp[1], ALU.subtract).then_inc(roped.sem, 1)
                tt(rot[:, :, HALF:HD], rtmp[2], rtmp[3], ALU.add).then_inc(roped.sem, 1)
                dve.wait_ge(*att_kept.at(n, 0))
                then(n, dve.tensor_copy(vrows[:, 1, :], att[:, 640:768]))
                dve.wait_ge(*gate_exp.at(n, 2))
                then(n, ts(col(S_EB, DH), col(S_EB, DH), 1.0, None, ALU.add))
                then(n, dve.reciprocal(col(S_BETA, DH), col(S_EB, DH)))
                then(n, ts(col(S_AX, DH), col(S_AX, DH), 0.0, None, ALU.max))
                then(n, tt(col(S_SP, DH), col(S_SP, DH), col(S_AX, DH), ALU.add))
                tt(col(S_G, DH), col(S_SP, DH), neg_a[:, :], ALU.mult).then_inc(g_ready.sem, 1)
                for k in range(1, TAPS):
                    for t in range(3 * DH):
                        if k == 1:
                            dve.wait_ge(*tap0.at(n, t + 1))
                        else:
                            dve.wait_ge(*conv_step.at(n, (k - 2) * 3 * DH + t + 1))
                        stt(out=convo[:, t, :], in0=conv3[:, t, k:k + P], scalar=conv_w[:, t * TAPS + k:t * TAPS + k + 1],
                            in1=convo[:, t, :], op0=ALU.mult, op1=ALU.add).then_inc(conv_step.sem, 1)
                dve.wait_ge(*conv_step.at(n, 3 * DH * (TAPS - 1)))
                dve.tensor_copy(conv3[:, :, 0:TAPS - 1], conv3[:, :, P:P + TAPS - 1]).then_inc(conv_tail.sem, 1)
                for i in range(4):
                    dve.wait_ge(*scored.at(n, i + 1))
                    stt(out=by_head(tile(A_P + i), 2), in0=by_head(bank[2 + i][:, :], 2), scalar=HD ** -0.5,
                        in1=over_heads(mask[:, :], 2), op0=ALU.mult, op1=ALU.add).then_inc(masked.sem, 1)
                dve.wait_ge(*masked.at(n, 4))
                then(n, dve.tensor_reduce(col(S_MAX, HEADS), arena[:, A_P * 512:(A_P + 4) * 512].rearrange("p (h c) -> p h c", h=HEADS),
                                          AX.X, ALU.max))
                then(n, tt(col(S_MAX, HEADS), col(S_MAX, HEADS), sinks[:, :], ALU.max))
                then(n, tt(col(S_SNK, HEADS), sinks[:, :], col(S_MAX, HEADS), ALU.subtract))
                ts(col(S_NMAX, HEADS), col(S_MAX, HEADS), -1.0, None, ALU.mult).then_inc(neg_max.sem, 1)
                then(n, dve.tensor_copy(mask[:, 0:P], C["band"][:, 0:P]))
                dve.wait_ge(*probs.at(n, 9))
                then(n, tt(col(S_DEN, HEADS), col(S_SUM, HEADS), col(S_SNK, HEADS), ALU.add))
                then(n, dve.reciprocal(col(S_RIN, HEADS), col(S_DEN, HEADS)))
                dve.wait_ge(*att_o.at(n, 1))
                dve.wait_ge(*stored.at(n, 0))
                tt(o_cat[:, 0:512].rearrange("p (h c) -> p h c", h=HEADS), bank[4][:, :].rearrange("p (h c) -> p h c", h=HEADS),
                   over_cols(col(S_RIN, HEADS), HD), ALU.mult).then_inc(att_out.sem, 1)
                dve.wait_ge(*g_ready.at(n, 1))
                tt(by_head(tile(A_UG)), over_heads(C["upto"], DH), over_cols(col(S_G, DH), P), ALU.mult).then_inc(g_ready.sem, 1)
                dve.wait_ge(*inv_norms.at(n, 1))
                tt(conv[:, 0:1024], conv[:, 0:1024], tile(A_SQ, 2), ALU.mult).then_inc(qk_normed.sem, 1)
                dve.wait_ge(*gc_copied.at(n, 2))
                then(n, tt(by_head(tile(A_DD)), by_head(bank[0][:, :]), over_cols(col(S_GC, DH), P), ALU.subtract))
                ts(tile(A_DI), tile(A_DD), 0.0, None, ALU.max).then_inc(diffs.sem, 1)
                ts(tile(A_DT), tile(A_DD), 0.0, None, ALU.min).then_inc(diffs.sem, 1)
                then(n, tt(col(S_BG, DH), col(S_BETA, DH), col(S_EGC, DH), ALU.mult))
                tt(col(S_KD, DH), col(S_GL, DH), col(S_GC, DH), ALU.subtract).then_inc(kd_pre.sem, 1)
                dve.wait_ge(*kd_exp.at(n, 1))
                dve.wait_ge(*ktok.at(n, 1))
                tt(by_head(tile(A_KBG)), by_head(bank[3][:, :]), over_cols(col(S_BG, DH), P), ALU.mult).then_inc(scaled.sem, 1)
                tt(by_head(tile(A_KDEC)), by_head(bank[3][:, :]), over_cols(col(S_KD, DH), P), ALU.mult).then_inc(scaled.sem, 1)
                dve.wait_ge(*decays.at(n, 1))
                then(n, tt(by_head(tile(A_DI)), by_head(tile(A_DI)), over_heads(C["strict"], DH), ALU.mult))
                then(n, tt(by_head(tile(A_DI)), by_head(tile(A_DI)), over_cols(col(S_BETA, DH), P), ALU.mult))
                dve.wait_ge(*ktok.at(n, 2))
                tt(tile(A_A), bank[5][:, :], tile(A_DI), ALU.mult).then_inc(a_ready.sem, 1)
                dve.wait_ge(*a_ready.at(n, 1))
                tt(by_head(tile(A_N)), by_head(tile(A_A)), over_heads(C["same16"], DH), ALU.mult)
                dve.wait_ge(*aT.at(n, 1))
                tt(by_head(tile(A_NT)), by_head(bank[0][:, :]), over_heads(C["same16"], DH), ALU.mult).then_inc(nT_ready.sem, 1)
                dve.wait_ge(*nT_ready.at(n, 1))
                stt(out=by_head(tile(A_R)), in0=by_head(tile(A_NT)), scalar=-1.0, in1=over_heads(C["ident"], DH),
                    op0=ALU.mult, op1=ALU.add).then_inc(x0_ready.sem, 1)
                dve.wait_ge(*ktok.at(n, 3))
                tt(by_head(tile(A_VB)), by_head(bank[4][:, :]), over_cols(col(S_BETA, DH), P), ALU.mult).then_inc(scaled.sem, 1)
                tt(by_head(tile(A_E32)), by_head(tile(A_A)), over_heads(C["off32"], DH), ALU.mult)
                tt(by_head(tile(A_E64)), by_head(tile(A_A)), over_heads(C["off64"], DH), ALU.mult)
                dve.wait_ge(*prod.at(n, 1))
                tt(tile(A_R), tile(A_R), bank[0][:, :], ALU.add).then_inc(prod_added.sem, 1)
                dve.wait_ge(*decays.at(n, 2))
                then(n, tt(by_head(tile(A_DT)), by_head(tile(A_DT)), over_heads(C["upto"], DH), ALU.mult))
                dve.wait_ge(*ktok.at(n, 4))
                tt(tile(A_QKT), bank[2][:, :], tile(A_DT), ALU.mult).then_inc(scaled.sem, 1)
                tt(tile(A_QDT), conv[:, 0:512], tile(A_EG), ALU.mult).then_inc(scaled.sem, 1)
                for k, b in ((1, 3), (2, 4)):
                    dve.wait_ge(*prod.at(n, k + 1))
                    dve.wait_ge(*prod_added.at(n, k))
                    tt(tile(A_R), tile(A_R), bank[b][:, :], ALU.add).then_inc(prod_added.sem, 1)
                for m, b in enumerate((1, 5)):
                    dve.wait_ge(*merge.at(n, m + 1))
                    tt(tile(A_R), tile(A_R), bank[b][:, :], ALU.subtract).then_inc(merged.sem, 1)
                for c, (bw, bk) in enumerate(((3, 4), (5, 1))):
                    rows = slice(c * CHUNK, (c + 1) * CHUNK)
                    dve.wait_ge(*w_state.at(n, c + 1))
                    tt(tile(A_VN)[rows, :], tile(A_U)[rows, :], bank[bw][rows, :], ALU.subtract).then_inc(v_new.sem, 1)
                    dve.wait_ge(*kv_done.at(n, c + 1))
                    dve.wait_ge(*o_done.at(n, c + 1))
                    last = (c + 1) * CHUNK - 1
                    for h in range(DH):
                        hs = slice(h * P, (h + 1) * P)
                        ins = stt(out=state[:, hs], in0=state[:, hs], scalar=tile(A_EG)[:, h * P + last:h * P + last + 1],
                                  in1=bank[bk][:, hs], op0=ALU.mult, op1=ALU.add)
                    ins.then_inc(state_new.sem, 1)
                dve.wait_ge(*o_copied.at(n, 2))
                then(n, tt(tile(A_DI), tile(A_O), tile(A_O), ALU.mult))
                then(n, dve.tensor_reduce(col(S_SS, DH), by_head(tile(A_DI)), AX.X, ALU.add))
                ts(col(S_SS, DH), col(S_SS, DH), 1.0 / DK, None, ALU.mult).then_inc(o_ms.sem, 1)
                then(n, tt(by_head(tile(A_O)), by_head(tile(A_O)), over_heads(norm_g[:, :], DH), ALU.mult))
                dve.wait_ge(*silu_done.at(n, 2))
                then(n, tt(tile(A_O), tile(A_O), z[:, :], ALU.mult))
                dve.wait_ge(*root.at(n, 1))
                refine(n, col(S_RT, DH), col(S_SS, DH), RMS_EPS, col(S_RT + 4, DH), DH)
                tt(by_head(o_cat[:, 512:1024]), by_head(tile(A_O)), over_cols(col(S_RT, DH), P), ALU.mult).then_inc(dn_out.sem, 1)
                dve.wait_ge(*x_loaded.at(n, 16))
                for i in range(2):
                    dve.wait_ge(*chunk_used.at(n, IN_CHUNKS + 2 * (i + 1)))
                    ins = stt(out=x1[:, i * 512:(i + 1) * 512], in0=x_in[:, i * 512:(i + 1) * 512], scalar=ALPHA,
                              in1=bank[3 + i][:, :], op0=ALU.mult, op1=ALU.add)
                ins.then_inc(residual.sem, 1)
                dve.wait_ge(*residual.at(n, 1))
                layer_norm(n, x1, ln1g, ln1b, x1, 2, lambda ins: ins.then_inc(x1_ready.sem, 1))
                for l in range(LISTS):
                    if l % 4 == 0:
                        dve.wait_ge(*key_scores_c.at(n, l // 4 + 1))
                    s = arena[:, A_S * 512 + l * KEYS:A_S * 512 + (l + 1) * KEYS]
                    a, b = slice(l * TOPK, l * TOPK + 8), slice(l * TOPK + 8, (l + 1) * TOPK)
                    alone(dve)
                    then(n, dve.max(best_v[:, a], s))
                    alone(dve)
                    dve.max_index(best_i[:, a], best_v[:, a], s)
                    then(n, dve.match_replace(s, best_v[:, a], s, LOWEST))
                    alone(dve)
                    then(n, dve.max(best_v[:, b], s))
                    alone(dve)
                    ins = dve.max_index(best_i[:, b], best_v[:, b], s)
                then(n, ins)
                then(n, dve.tensor_copy(best_if[:, :], best_i[:, :]))
                bv = best_v[:, :].rearrange("p (h s k) -> p h s k", s=2, k=TOPK)
                bi = best_if[:, :].rearrange("p (h s k) -> p h s k", s=2, k=TOPK)
                cube = [P, PH, TOPK, TOPK]
                hot = arena[:, A_HOT * 512:(A_HOT + 4) * 512].rearrange("p (h k i) -> p h k i", h=PH, k=TOPK)
                for h in range(PH):
                    cd = arena[:, A_CAND * 512 + h * 256:A_CAND * 512 + (h + 1) * 256]
                    ins = tt(cd.rearrange("p (a b) -> p a b", a=TOPK), bv[:, h, 0, :].unsqueeze(2).to_broadcast([P, TOPK, TOPK]),
                             bv[:, h, 1, :].unsqueeze(1).to_broadcast([P, TOPK, TOPK]), ALU.add)
                then(n, ins)
                for h in range(PH):
                    cd = arena[:, A_CAND * 512 + h * 256:A_CAND * 512 + (h + 1) * 256]
                    a, b = slice(h * TOPK, h * TOPK + 8), slice(h * TOPK + 8, (h + 1) * TOPK)
                    alone(dve)
                    then(n, dve.max(top_v[:, a], cd))
                    alone(dve)
                    dve.max_index(top_p[:, a], top_v[:, a], cd)
                    then(n, dve.match_replace(cd, top_v[:, a], cd, LOWEST))
                    alone(dve)
                    then(n, dve.max(top_v[:, b], cd))
                    alone(dve)
                    ins = dve.max_index(top_p[:, b], top_v[:, b], cd)
                then(n, ins)
                tv = top_v[:, :].rearrange("p (h k) -> p h k", h=PH)
                gt = gate[:, :].rearrange("p (h k) -> p h k", h=PH)
                tt(gt, tv, tv[:, :, 0:1].to_broadcast([P, PH, TOPK]), ALU.subtract).then_inc(best_sub.sem, 1)
                then(n, ts(pos_u[:, :], top_p[:, :], 4, None, ALU.logical_shift_right))
                then(n, dve.tensor_copy(pos_hi[:, :], pos_u[:, :]))
                then(n, ts(pos_u[:, :], top_p[:, :], TOPK - 1, None, ALU.bitwise_and))
                then(n, dve.tensor_copy(pos_lo[:, :], pos_u[:, :]))
                for side, pos_s in enumerate((pos_hi, pos_lo)):
                    for h in range(PH):
                        ph = pos_s[:, h * TOPK:(h + 1) * TOPK]
                        ins = tt(hot[:, h], over_heads(C["iota"], TOPK), over_cols(ph, TOPK), ALU.is_equal)
                    then(n, ins)
                    for h in range(PH):
                        ins = tt(hot[:, h], hot[:, h], bi[:, h, side, :].unsqueeze(1).to_broadcast([P, TOPK, TOPK]), ALU.mult)
                    then(n, ins)
                    then(n, dve.tensor_reduce(pos_s[:, :], hot.rearrange("p h k i -> p (h k) i"), AX.X, ALU.add))
                then(n, stt(out=pos_hi[:, :], in0=pos_hi[:, :], scalar=float(KEYS), in1=pos_lo[:, :], op0=ALU.mult, op1=ALU.add))
                dve.tensor_copy(expert[:, :], pos_hi[:, :]).then_inc(chosen.sem, 1)
                dve.wait_ge(*best_exp.at(n, 1))
                then(n, dve.tensor_reduce(col(S_GS, PH), gt, AX.X, ALU.add))
                then(n, dve.reciprocal(col(S_GR, PH), col(S_GS, PH)))
                tt(gt, gt, over_cols(col(S_GR, PH), TOPK), ALU.mult).then_inc(chosen.sem, 1)
                dve.wait_ge(*chosen.at(n, 2))
                for q in range(SLOTS // GROUPED):
                    for j in range(q * GROUPED, (q + 1) * GROUPED):
                        dve.wait_ge(*gathered[j % RING].at(n, 16 * (j // RING + 1)))
                        u = ring3[:, j % RING, 0:D]
                        dve.tensor_tensor_reduce(u, u, x1[:, :], 1.0, 0.0, ALU.mult, ALU.add, h_raw[:, j:j + 1]).then_inc(dotted.sem, 1)
                    s = slice(q * GROUPED, (q + 1) * GROUPED)
                    dve.wait_ge(*gelued.at(n, q + 1))
                    tt(h_w[:, s], h_raw[:, s], gate[:, s], ALU.mult).then_inc(weighted.sem, 1)
                dve.wait_ge(*added.at(n, SLOTS))
                for i in range(2):
                    ins = stt(out=x1[:, i * 512:(i + 1) * 512], in0=x1[:, i * 512:(i + 1) * 512], scalar=ALPHA,
                              in1=expert_sum[i][:, :], op0=ALU.mult, op1=ALU.add)
                then(n, ins)
                layer_norm(n, x1, ln2g, ln2b, o_cat, 3, lambda ins: ins.then_inc(out_ready.sem, 1))
            assert steps[0] == DVE_STEPS, steps


def chunked(w):
    d, m = w.shape
    return np.ascontiguousarray(w.reshape(d // P, P, m // W, W).transpose(2, 1, 0, 3)).reshape(m // W, P, -1)


def by_partition(a):
    return np.ascontiguousarray(a.reshape(-1, P, a.shape[1]).transpose(1, 0, 2)).reshape(P, -1)


def kernel(**inputs):
    import concourse.bacc as bacc
    from concourse.bass_utils import run_bass_kernel_spmd

    a = {k: np.asarray(v) for k, v in inputs.items()}
    x = a["x"].reshape(SEQ, D)
    w_in = a["w_in"]
    qkv, dn = HEADS * HD + 2 * KV * HD, DH * DK
    b_at = qkv + 3 * dn
    z_at = b_at + 2 * DH
    w_main = np.concatenate([w_in[:, :b_at], w_in[:, z_at:]], axis=1)
    arrays = {
        "consts": constants(),
        "weights": np.concatenate([chunked(w_main), chunked(a["w_out"]), chunked(a["peer_w_query"])], axis=0),
        "w_ba": by_partition(w_in[:, b_at:z_at]),
        "sub_keys": np.ascontiguousarray(a["peer_sub_keys"].transpose(3, 0, 1, 2)).reshape(P, -1),
        "conv_w": np.ascontiguousarray(a["conv_w"].reshape(TAPS, 3 * DH, P).transpose(2, 1, 0)).reshape(P, -1),
        "xT": np.ascontiguousarray(x.reshape(NB, P, KT, P).transpose(0, 3, 2, 1)).reshape(NB, P, D),
        "x": x.reshape(NB, P, D),
        "positions": np.ascontiguousarray(a["positions"].reshape(NB, P).T.astype(np.int32)),
        "uv": np.concatenate([a["peer_u"], a["peer_v"]], axis=1),
    }
    for k in ("ln1_g", "ln1_b", "ln2_g", "ln2_b", "a_log", "dt_bias", "dn_norm_g", "attn_sinks"):
        arrays[k] = a[k]
    nc = bacc.Bacc("TRN2", target_bir_lowering=False, num_devices=1)
    io = {k: nc.dram_tensor(f"in_{k}", v.shape, mybir.dt.from_np(v.dtype), kind="ExternalInput").ap() for k, v in arrays.items()}
    io["out"] = nc.dram_tensor("out_0", (NB, P, D), F32, kind="ExternalOutput").ap()
    build(nc, io)
    r = run_bass_kernel_spmd(nc, [{f"in_{k}": v for k, v in arrays.items()}], core_ids=[0])
    return r.results[0]["out_0"].reshape(1, SEQ, D)
```

```python
import math
from contextlib import ExitStack

import numpy as np

import concourse.bass as bass
from concourse import mybir
from concourse.alu_op_type import AluOpType as ALU

ACT = mybir.ActivationFunctionType
AX = mybir.AxisListType
F32, I32, U32 = mybir.dt.float32, mybir.dt.int32, mybir.dt.uint32

P = 128
SEQ, D = 1024, 1024
NB = SEQ // P
KT = D // P
HEADS, KV, HD = 8, 2, 64
GROUP = HEADS // KV
HALF = HD // 2
DH, DK = 4, 128
CHUNK = 64
TAPS = 4
PH, KEYS, TOPK = 8, 128, 16
LISTS = 2 * PH
SLOTS = PH * TOPK
ALPHA = 2.0 ** 0.25
LN_EPS, RMS_EPS, L2_EPS = 1e-5, 1e-6, 1e-6
NEG = -1e30
LOWEST = -3e38
W = 256
IN_CHUNKS = (HEADS * HD + 2 * KV * HD + 4 * DH * DK) // W
OUT_CHUNKS = D // W
Q_CHUNKS = LISTS * P // W
CHUNKS = IN_CHUNKS + OUT_CHUNKS + Q_CHUNKS
RING = 8
PAIRS = SLOTS // 2
STAGED = 112
DIAGS = 4
KEPT = 3
EARLY = 2 + RING * 2 * D // (KT * W)
TWO_PI = (6.28125, 2029.0 / 2 ** 20, 2 * math.pi - 6.28125 - 2029.0 / 2 ** 20)

CONSTS = {}
_at = 0
for _name, _width in (("ident", P), ("ones", P), ("upto", P), ("strict", P), ("same16", P), ("off32", P),
                      ("off64", P), ("same64", P), ("band", 2 * P), ("iota", TOPK),
                      ("freq", HALF), ("eps_ln", 1), ("eps_rms", 1), ("eps_l2", 1), ("ln_qscale", 1)):
    CONSTS[_name] = (_at, _at + _width)
    _at += _width
CONST_COLS = _at


def constants():
    i, j = np.arange(P)[:, None], np.arange(P)[None, :]
    same = lambda w: (i // w) == (j // w)
    c = np.arange(2 * P)[None, :]
    full = lambda v: np.full((P, 1), v)
    row = lambda v: np.broadcast_to(np.asarray(v)[None, :], (P, len(v)))
    parts = {
        "ident": i == j, "ones": np.ones((P, P)),
        "upto": (i <= j) & same(CHUNK),
        "strict": (i > j) & same(CHUNK),
        "same16": same(16), "off32": same(32) & ~same(16), "off64": same(64) & ~same(32),
        "same64": same(CHUNK),
        "band": np.where((c > i) & (c <= i + P), 0.0, NEG),
        "iota": row(np.arange(TOPK)),
        "freq": row(np.float32(10000.0) ** (-np.arange(HALF, dtype=np.float32) / np.float32(HALF))),
        "eps_ln": full(LN_EPS), "eps_rms": full(RMS_EPS), "eps_l2": full(L2_EPS),
        "ln_qscale": full(math.log(DK ** -0.5)),
    }
    return np.concatenate([np.asarray(parts[k], np.float32) for k in CONSTS], axis=1)


STEPS = dict(
    q=1, kv=1, conv_q=1, turn_qk=1, conv_k=1, conv_v=1, z=1, scores=1, softmax=1, turn_p=1, att_o=1,
    norms=1, decay=1, kk=1, aT=1, pow2=1, pow4=1, pow8=1, prod3=1, turn32=1, merge32=1, turn64=1,
    merge64=1, solve=1, ws0=1, kv0=1, ws1=1, kv1=1, dn=1, o_T=1, out0=2, out1=2, x1_T=1,
    qu0=2, top0=1, sel0=2, qu1=2, top1=1, sel1=3, qu2=2, top2=1, sel2=2, qu3=2, top3=1, sel3=3,
    pick0=2, pick1=1,
)
assert 2 * sum(STEPS.values()) >= STAGED + RING


class Marks:

    def __init__(self, pairs=None, behind={}):
        self.names, self.pairs, self.behind, self.done = list(STEPS), pairs, behind, 0

    def __call__(self, name):
        assert self.names.pop(0) == name
        if self.pairs:
            self.pairs(self.done, self.done + STEPS[name])
            self.done += STEPS[name]
        if name in self.behind:
            self.behind[name]()


class Signal:

    def __init__(self, sem, per_block, before):
        self.sem, self.per_block, self.before = sem, per_block, before

    def at(self, n, k):
        assert k + self.before > 0
        return self.sem, n * self.per_block + (k + self.before)


def build(nc, io):
    ctx = ExitStack()
    with ctx:
        def sb(name, cols, dt=F32, parts=P):
            return ctx.enter_context(nc.sbuf_tensor(name, [parts, cols], dt))

        def sem(name):
            return ctx.enter_context(nc.semaphore(name))

        def signal(name, per_block=1, before=0):
            return Signal(sem(name), per_block, before)

        bank = [ctx.enter_context(nc.psum_tensor(f"bank{i}", [P, 512], F32)) for i in range(6)]
        expert_sum = [ctx.enter_context(nc.psum_tensor(f"expert_sum{i}", [P, 512], F32)) for i in range(2)]

        const = sb("const", CONST_COLS)
        C = {k: const[:, a:b] for k, (a, b) in CONSTS.items()}
        w_ba = sb("w_ba", KT * 2 * DH)
        sub_keys = sb("sub_keys", LISTS * KEYS)
        conv_w = sb("conv_w", 3 * DH * TAPS)
        neg_a = sb("neg_a", DH)
        dt_b = sb("dt_b", DH)
        norm_g = sb("norm_g", DK)
        sinks = sb("sinks", HEADS)
        cos = sb("cos", NB * HALF)
        sin = sb("sin", NB * HALF)
        mask = sb("mask", 2 * P)

        state = sb("state", DH * DK)
        k_keys = sb("k_keys", KV * 2 * P)
        LN_ROWS = slice(HD, HD + 8)
        v_rows = sb("v_rows", 2 * KV * HD)
        conv_in = sb("conv_in", 3 * DH * (P + TAPS - 1))

        chunk = [sb(f"chunk{i}", KT * W) for i in range(2)]
        ring = sb("ring", RING * 2 * D)
        xT = sb("xT", KT * P)
        kept = sb("kept", KEPT * KT * W)

        conv = sb("conv", 3 * DH * P)
        z = sb("z", DH * DK)
        o_cat = sb("o_cat", D)
        oT = sb("oT", KT * P)
        x1 = sb("x1", D)
        x1_used = sb("x1_used", D)
        gate_used = sb("gate_used", SLOTS)
        expert_used = sb("expert_used", SLOTS, U32)
        small = sb("small", 256)
        tiles = 20
        arena = sb("arena", tiles * 512)
        expert = sb("expert", SLOTS, U32)
        gate = sb("gate", SLOTS)
        h_raw = sb("h_raw", SLOTS)
        h_w = sb("h_w", SLOTS)
        diag = sb("diag", DIAGS * P)

        def tile(i, k=1):
            return arena[:, i * 512:(i + k) * 512]

        def by_head(ap, h=DH):
            return ap.rearrange("p (h c) -> p h c", h=h)

        def col(i, k=1):
            return small[:, i:i + k]

        def over_cols(ap, k):
            return ap.unsqueeze(2).to_broadcast([P, ap.shape[1], k])

        def over_heads(ap, h):
            return ap.unsqueeze(1).to_broadcast([P, h, ap.shape[1]])

        S_BETA, S_EB, S_AX, S_NX, S_MN, S_SP, S_G, S_GC, S_GL, S_EGC, S_BG, S_KD = (4 * i for i in range(12))
        S_MAX, S_NMAX, S_SUM, S_SNK, S_DEN, S_RIN = (48 + 8 * i for i in range(6))
        S_SS, S_VE, S_LN, S_R, S_T = (96 + 4 * i for i in range(5))
        S_LN1, S_OUT = 120, 200
        S_GM, S_GS, S_GR = 160, 168, 176
        S_RT = 184

        setup_in = sem("setup_in")
        late_in = sem("late_in")
        kept_in = [sem(f"kept_in{i}") for i in range(KEPT)]
        early_in = [sem(f"early_in{i}") for i in range(EARLY)]
        passed = sem("passed")
        setup_steps = sem("setup_steps")
        angles = sem("angles")
        tables = sem("tables")
        neg_a_ready = sem("neg_a_ready")

        xT_in = signal("xT_in", 16)
        x_loaded = signal("x_loaded", 16)
        chunk_in = [signal(f"chunk_in{i}", 16 * ((CHUNKS - KEPT) // 2)) for i in range(2)]
        chunk_used = signal("chunk_used", CHUNKS, before=1)
        att_copied = signal("att_copied", 2)
        conv_copied = signal("conv_copied", 3)
        z_copied = signal("z_copied", 1)
        roped = signal("roped", 2)
        att_T = signal("att_T", 2)
        att_Tc = signal("att_Tc", 3)
        scored = signal("scored", 4)
        masked = signal("masked", 4)
        neg_max = signal("neg_max", 1)
        probs = signal("probs", 9)
        probs_T = signal("probs_T", 4)
        probs_Tc = signal("probs_Tc", 4)
        att_o = signal("att_o", 1)
        att_kept = signal("att_kept", 1, before=1)
        att_out = signal("att_out", 1)
        tap0 = signal("tap0", 3 * DH)
        conv_step = signal("conv_step", 3 * DH * (TAPS - 1))
        conv_tail = signal("conv_tail", 1, before=1)
        silu_done = signal("silu_done", 1)
        squares = signal("squares", 1)
        norms = signal("norms", 2)
        inv_norms = signal("inv_norms", 1)
        qk_normed = signal("qk_normed", 1)
        gate_pre = signal("gate_pre", 1)
        gate_exp = signal("gate_exp", 1)
        g_ready = signal("g_ready", 2)
        g_sums = signal("g_sums", 2)
        gc_copied = signal("gc_copied", 2)
        kd_pre = signal("kd_pre", 1)
        kd_exp = signal("kd_exp", 1)
        diffs = signal("diffs", 2)
        decays = signal("decays", 2)
        ktok = signal("ktok", 4)
        a_ready = signal("a_ready", 1)
        aT = signal("aT", 1)
        nT_ready = signal("nT_ready", 1)
        x0_ready = signal("x0_ready", 1)
        sq = signal("sq", 5)
        sq_copied = signal("sq_copied", 5)
        prod = signal("prod", 3)
        prod_added = signal("prod_added", 3)
        turn = signal("turn", 4)
        turn_copied = signal("turn_copied", 4)
        merge = signal("merge", 2)
        merged = signal("merged", 2)
        scaled = signal("scaled", 5)
        solved = signal("solved", 2)
        solved_copied = signal("solved_copied", 2)
        w_state = signal("w_state", 2)
        v_new = signal("v_new", 2)
        o_done = signal("o_done", 2)
        kv_done = signal("kv_done", 2)
        state_new = signal("state_new", 2, before=1)
        o_copied = signal("o_copied", 2)
        o_squares = signal("o_squares", 1)
        o_ms = signal("o_ms", 1)
        root = signal("root", 2)
        root_out = signal("root_out", 1)
        dn_out = signal("dn_out", 1)
        o_T = signal("o_T", 2)
        o_Tc = signal("o_Tc", 2)
        residual = signal("residual", 1)
        ln1_rows = signal("ln1_rows", 2)
        ln2_rows = signal("ln2_rows", 2)
        var_ready = signal("var_ready", 1)
        var_out = signal("var_out", 1)
        x1_ready = signal("x1_ready", 1)
        x1_T = signal("x1_T", 2)
        x1_Tc = signal("x1_Tc", 2)
        queries_c = signal("queries_c", 4)
        key_scores = signal("key_scores", 4)
        key_scores_c = signal("key_scores_c", 4, before=1)
        best_sub = signal("best_sub", 1)
        best_exp = signal("best_exp", 1)
        chosen = signal("chosen", 2, before=1)
        gathered = [signal(f"gathered{i}", 16 * len(range(i, SLOTS, RING))) for i in range(RING)]
        dotted = signal("dotted", SLOTS)
        gelued = signal("gelued", PAIRS)
        weighted = signal("weighted", SLOTS)
        rows_staged = signal("rows_staged", 1, before=1)
        diag_ready = signal("diag_ready", SLOTS)
        added = signal("added", SLOTS, before=RING)
        sums_read = signal("sums_read", 1, before=1)
        out_ready = signal("out_ready", 1, before=2)
        staged = signal("staged", 2)
        stored = signal("stored", 16, before=32)
        DVE_STEPS, ACT_STEPS, LN_STEPS = 76, 6, 7
        dve_done = signal("dve_done", DVE_STEPS)
        act_done = signal("act_done", ACT_STEPS)
        dve_out_done = signal("dve_out_done", LN_STEPS)
        act_out_done = signal("act_out_done", 1)

        LN1_G, LN1_B = (bank[0], bank[5]), (bank[1], bank[2])
        LN2_G, LN2_B = (bank[4], bank[5]), (bank[2], bank[3])

        conv3 = conv_in[:, :].rearrange("p (t c) -> p t c", t=3 * DH)
        convo = conv[:, :].rearrange("p (t c) -> p t c", t=3 * DH)
        keysT = k_keys[0:HD, :].rearrange("p (g c) -> p g c", g=KV)
        vrows = v_rows[:, :].rearrange("p (s c) -> p s c", s=2)
        ring3 = ring[:, :].rearrange("p (r c) -> p r c", r=RING)

        A_ROT, A_T = 16, 10
        A_QT = 8
        A_P, A_PT = 0, 4
        A_ATT = 14
        att = arena[:, A_ATT * 512:(A_ATT + 2) * 512]
        A_SQ = 12
        (A_UG, A_EG, A_DD, A_DI, A_DT, A_A, A_NT, A_E32, A_E64, A_R, A_N2, A_N2T, A_N4, A_N4T, A_N8,
         A_KBG, A_KDEC, A_VB, A_QKT, A_QDT) = range(tiles)
        A_Z, A_TT, A_U, A_WT, A_VN = A_N2, A_N2T, A_N4, A_N4T, A_N8
        A_N, A_O = A_UG, A_DD
        A_QP, A_S, A_CAND, A_HOT, A_BEST = 0, 4, 8, 12, 16
        best = [arena[:, (A_BEST * 512 + i * LISTS * TOPK):(A_BEST * 512 + (i + 1) * LISTS * TOPK)] for i in range(3)]
        best_v, best_i, best_if = best[0], best[1].bitcast(U32), best[2]
        top = [arena[:, (A_BEST + 2) * 512 + i * SLOTS:(A_BEST + 2) * 512 + (i + 1) * SLOTS] for i in range(5)]
        top_v, top_p, pos_hi, pos_lo, pos_u = top[0], top[1].bitcast(U32), top[2], top[3], top[4].bitcast(U32)

        rot = arena[:, A_ROT * 512:A_ROT * 512 + 640].rearrange("p (h c) -> p h c", c=HD)
        rtmp = [arena[:, A_T * 512 + 320 * i:A_T * 512 + 320 * (i + 1)].rearrange("p (h c) -> p h c", c=HALF)
                for i in range(4)]

        positions_in = arena[:, 0:NB].bitcast(I32)
        block = ctx.enter_context(nc.Block())
        setup, late = 16 * 8, 16 * 2

        def kept_chunk(c):
            return kept[:, c * KT * W:(c + 1) * KT * W]

        def early_place(c):
            i = (c - KEPT) % EARLY
            return chunk[i][:, :] if i < 2 else ring[:, (i - 2) * KT * W:(i - 1) * KT * W]

        def alone(eng):
            eng.sem_inc(passed, 1)

        @block.sync
        def _(sp):
            sp.sem_inc(stored.sem, 32)
            sp.dma_start(xT[:, :], io["xT"][0]).then_inc(xT_in.sem, 16)
            sp.dma_start(kept_chunk(0), io["weights"][0]).then_inc(kept_in[0], 16)
            for dst, src in ((w_ba, io["w_ba"]), (const, io["consts"])):
                sp.dma_start(dst[:, :], src).then_inc(setup_in, 16)
            for c in range(1, KEPT):
                sp.dma_start(kept_chunk(c), io["weights"][c]).then_inc(kept_in[c], 16)
            for c in range(KEPT, CHUNKS):
                if c >= KEPT + EARLY:
                    sp.wait_ge(*chunk_used.at(0, c - EARLY + 1))
                if c == IN_CHUNKS:
                    sp.dma_start(x1[:, :], io["x"][0]).then_inc(x_loaded.sem, 16)
                sp.dma_start(early_place(c), io["weights"][c]).then_inc(early_in[(c - KEPT) % EARLY], 16)
            for i in range(2):
                sp.sem_inc(chunk_in[i].sem, chunk_in[i].per_block)
            with sp.Fori(1, NB) as n:
                sp.wait_ge(*chunk_used.at(n, 0))
                alone(sp)
                sp.dma_start(xT[:, :], io["xT"][bass.ds(n, 1), :, :].rearrange("n p c -> (n p) c")).then_inc(xT_in.sem, 16)
                for c in range(KEPT, CHUNKS):
                    if c == IN_CHUNKS:
                        sp.wait_ge(*rows_staged.at(n, 0))
                        alone(sp)
                        sp.dma_start(x1[:, :], io["x"][bass.ds(n, 1), :, :].rearrange("n p c -> (n p) c")).then_inc(x_loaded.sem, 16)
                    sp.wait_ge(*chunk_used.at(n, c - 1 if c > KEPT + 1 else 0))
                    alone(sp)
                    sp.dma_start(chunk[c % 2][:, :], io["weights"][c]).then_inc(chunk_in[c % 2].sem, 16)
            sp.wait_ge(*stored.at(NB, 0))

        def ring_free(j):
            before = j - RING if j >= RING else (SLOTS - 1 - (SLOTS - 1 - j) % RING) - SLOTS
            return before + 1

        def arrived(j):
            return 16 * (j // RING + 1)

        @block.gpsimd
        def _(pool):
            with pool.Fori(0, NB) as n:
                for j in range(SLOTS):
                    if j in (0, STAGED):
                        pool.wait_ge(*staged.at(n, 1 + (j > 0)))
                        alone(pool)
                    pool.wait_ge(*added.at(n, ring_free(j)))
                    alone(pool)
                    pool.indirect_dma_start(
                        out=ring[:, (j % RING) * 2 * D:(j % RING + 1) * 2 * D], out_offset=None, in_=io["uv"],
                        in_offset=bass.IndirectOffsetOnAxis(ap=expert_used[:, j:j + 1], axis=0),
                    ).then_inc(gathered[j % RING].sem, 16)

        @block.tensor
        def _(pe):
            ident = C["ident"]
            xTv = xT[:, :].rearrange("p (k c) -> p k c", k=KT)
            oTv = oT[:, :].rearrange("p (k c) -> p k c", k=KT)
            ch = [c[:, :].rearrange("p (k c) -> p k c", k=KT) for c in chunk]
            ba = w_ba[:, :].rearrange("p (k c) -> p k c", k=KT)
            sk = sub_keys[:, :].rearrange("p (l c) -> p l c", l=LISTS)

            def use_chunk(n, c, early):
                if c < KEPT:
                    if early:
                        pe.wait_ge(kept_in[c], 16)
                    return kept_chunk(c).rearrange("p (k c) -> p k c", k=KT)
                if early:
                    pe.wait_ge(early_in[(c - KEPT) % EARLY], 16 * ((c - KEPT) // EARLY + 1))
                    return early_place(c).rearrange("p (k c) -> p k c", k=KT)
                pe.wait_ge(*chunk_in[c % 2].at(n, 16 * ((c - KEPT) // 2 + 1)))
                return ch[c % 2]

            def tokens_out(n, c, out, act, early):
                w = use_chunk(n, c, early)
                for k in range(KT):
                    mm = pe.matmul(out, act[:, k, :], w[:, k, :], start=(k == 0), stop=(k == KT - 1))
                mm.then_inc(chunk_used.sem, 1)

            def channels_out(n, c, outs, act, early):
                w = use_chunk(n, c, early)
                for i, out in enumerate(outs):
                    for k in range(KT):
                        mm = pe.matmul(out, w[:, k, i * P:(i + 1) * P], act[:, k, :], start=(k == 0), stop=(k == KT - 1))
                mm.then_inc(chunk_used.sem, 1)

            def each_head(out, lhsT, rhs):
                for h in range(DH):
                    hs = slice(h * P, (h + 1) * P)
                    mm = pe.matmul(out[:, hs], lhsT[:, hs], rhs[:, hs], start=True, stop=True)
                return mm

            def turn_each(out, in_, k=4, parts=P):
                for h in range(k):
                    mm = pe.transpose(out[:, h * P:(h + 1) * P], in_[:, h * P:(h + 1) * P], ident)
                return mm

            pe.sem_inc(chunk_used.sem, 1)
            pe.sem_inc(added.sem, RING)

            def ln_row(banks, row, done):
                for i in range(2):
                    k = HD + 2 * row + i
                    mm = pe.matmul(banks[i][:, :], ident[LN_ROWS, k:k + 1].to_broadcast([8, P]), k_keys[LN_ROWS, :], start=True, stop=True)
                mm.then_inc(done.sem, 1)

            def mix(n, mark, early=False):
                pe.wait_ge(*xT_in.at(n, 16))
                pe.wait_ge(*key_scores_c.at(n, 0))
                tokens_out(n, 0, bank[0][:, 0:W], xTv, early)
                tokens_out(n, 1, bank[0][:, W:2 * W], xTv, early)
                mark("q")
                pe.wait_ge(setup_in, setup)
                for k in range(KT):
                    pe.matmul(bank[1][:, W:W + 2 * DH], xTv[:, k, :], ba[:, k, :], start=(k == 0), stop=(k == KT - 1))
                tokens_out(n, 2, bank[1][:, 0:W], xTv, early)
                mark("kv")

                def conv_channels(t):
                    for i in range(2):
                        channels_out(n, 3 + 2 * t + i, [bank[3 + t][:, (2 * i + j) * P:(2 * i + j + 1) * P] for j in range(2)], xTv, early)

                pe.wait_ge(*out_ready.at(n, -1))
                conv_channels(0)
                mark("conv_q")
                pe.wait_ge(*roped.at(n, 2))
                pe.wait_ge(*att_copied.at(n, 2))
                alone(pe)
                for h in range(HEADS):
                    mm = pe.transpose(bank[h // 4][0:HD, (h % 4) * P:(h % 4 + 1) * P], rot[:, h, :], ident)
                mm.then_inc(att_T.sem, 1)
                for g in range(KV):
                    mm = pe.transpose(bank[2][0:HD, g * P:(g + 1) * P], rot[:, HEADS + g, :], ident)
                mm.then_inc(att_T.sem, 1)
                mark("turn_qk")
                conv_channels(1)
                mark("conv_k")
                conv_channels(2)
                mark("conv_v")
                pe.wait_ge(*att_Tc.at(n, 3))
                tokens_out(n, 9, bank[2][:, 0:W], xTv, early)
                tokens_out(n, 10, bank[2][:, W:2 * W], xTv, early)
                mark("z")
                pe.wait_ge(*z_copied.at(n, 1))
                pe.wait_ge(*conv_copied.at(n, 3))
                for h in range(HEADS):
                    mm = pe.matmul(bank[2 + h // 2][:, (h % 2) * 2 * P:(h % 2 + 1) * 2 * P],
                                   arena[0:HD, A_QT * 512 + h * P:A_QT * 512 + (h + 1) * P], keysT[:, h // GROUP, :],
                                   start=True, stop=True)
                    if h % 2:
                        mm.then_inc(scored.sem, 1)
                mark("scores")
                mark("softmax")
                pe.wait_ge(*masked.at(n, 4))
                for h in range(HEADS):
                    pe.wait_ge(*probs.at(n, h + 1))
                    for s in range(2):
                        i = 2 * h + s
                        mm = pe.transpose(bank[i // 4][:, (i % 4) * P:(i % 4 + 1) * P],
                                          arena[:, A_P * 512 + i * P:A_P * 512 + (i + 1) * P], ident)
                    if h % 2:
                        mm.then_inc(probs_T.sem, 1)
                mark("turn_p")
                for h in range(HEADS):
                    if h % 2 == 0:
                        pe.wait_ge(*probs_Tc.at(n, h // 2 + 1))
                    g = h // GROUP
                    for s in range(2):
                        i = 2 * h + s
                        mm = pe.matmul(bank[4][:, h * HD:(h + 1) * HD], arena[:, A_PT * 512 + i * P:A_PT * 512 + (i + 1) * P],
                                       vrows[:, s, g * HD:(g + 1) * HD], start=(s == 0), stop=(s == 1))
                mm.then_inc(att_o.sem, 1)
                mark("att_o")

                pe.wait_ge(*squares.at(n, 1))
                for i in range(2):
                    pe.matmul(bank[2 + i][:, :], C["ones"], tile(A_SQ + i), start=True, stop=True).then_inc(norms.sem, 1)
                pe.wait_ge(*g_ready.at(n, 2))
                pe.matmul(bank[1][:, 0:DH], C["upto"], col(S_G, DH), start=True, stop=True)
                pe.matmul(bank[1][:, DH:2 * DH], C["same64"], col(S_G, DH), start=True, stop=True).then_inc(g_sums.sem, 1)
                pe.matmul(bank[0][:, :], C["ones"], tile(A_UG), start=True, stop=True).then_inc(g_sums.sem, 1)
                mark("norms")
                mark("decay")
                pe.wait_ge(*qk_normed.at(n, 1))
                qn, kn, vn = (conv[:, i * 512:(i + 1) * 512] for i in range(3))
                pe.wait_ge(*inv_norms.at(n, 1))
                turn_each(bank[3], kn).then_inc(ktok.sem, 1)
                each_head(bank[5], kn, kn).then_inc(ktok.sem, 1)
                pe.wait_ge(*att_out.at(n, 1))
                turn_each(bank[4], vn).then_inc(ktok.sem, 1)
                each_head(bank[2], kn, qn).then_inc(ktok.sem, 1)
                mark("kk")
                pe.wait_ge(*a_ready.at(n, 1))
                pe.wait_ge(*decays.at(n, 2))
                turn_each(bank[0], tile(A_A)).then_inc(aT.sem, 1)
                mark("aT")
                pe.wait_ge(*nT_ready.at(n, 1))
                each_head(bank[1], tile(A_NT), tile(A_N)).then_inc(sq.sem, 1)
                pe.wait_ge(*scaled.at(n, 2))
                each_head(bank[3], tile(A_N), tile(A_NT)).then_inc(sq.sem, 1)
                mark("pow2")
                pe.wait_ge(*sq_copied.at(n, 2))
                pe.wait_ge(*scaled.at(n, 3))
                each_head(bank[4], tile(A_N2T), tile(A_N2)).then_inc(sq.sem, 1)
                each_head(bank[5], tile(A_N2), tile(A_N2T)).then_inc(sq.sem, 1)
                pe.wait_ge(*x0_ready.at(n, 1))
                each_head(bank[0], tile(A_N2), tile(A_R)).then_inc(prod.sem, 1)
                mark("pow4")
                pe.wait_ge(*sq_copied.at(n, 4))
                each_head(bank[1], tile(A_N4T), tile(A_N4)).then_inc(sq.sem, 1)
                pe.wait_ge(*prod_added.at(n, 1))
                each_head(bank[3], tile(A_N4), tile(A_R)).then_inc(prod.sem, 1)
                mark("pow8")
                pe.wait_ge(*sq_copied.at(n, 5))
                pe.wait_ge(*prod_added.at(n, 2))
                each_head(bank[4], tile(A_N8), tile(A_R)).then_inc(prod.sem, 1)
                mark("prod3")
                for m, (e, b) in enumerate(((A_E32, (5, 0, 1)), (A_E64, (3, 4, 5)))):
                    if m == 0:
                        pe.wait_ge(*prod_added.at(n, 3))
                    else:
                        pe.wait_ge(*merged.at(n, 1))
                    each_head(bank[b[0]], tile(e), tile(A_R)).then_inc(turn.sem, 1)
                    turn_each(bank[b[1]], tile(A_R)).then_inc(turn.sem, 1)
                    mark(("turn32", "turn64")[m])
                    pe.wait_ge(*turn_copied.at(n, 2 * m + 2))
                    each_head(bank[b[2]], tile(A_TT), tile(A_Z)).then_inc(merge.sem, 1)
                    mark(("merge32", "merge64")[m])
                pe.wait_ge(*merged.at(n, 2))
                each_head(bank[0], tile(A_R), tile(A_VB)).then_inc(solved.sem, 1)
                each_head(bank[1], tile(A_KBG), tile(A_R)).then_inc(solved.sem, 1)
                mark("solve")
                pe.wait_ge(*solved_copied.at(n, 2))
                pe.wait_ge(*scaled.at(n, 5))
                for c, (bw, bo, bk) in enumerate(((3, 2, 4), (5, 0, 1))):
                    rows = slice(c * CHUNK, (c + 1) * CHUNK)
                    if c == 0:
                        pe.wait_ge(*state_new.at(n, 0))
                    else:
                        pe.wait_ge(*state_new.at(n, 1))
                    each_head(bank[bw], tile(A_WT), state[:, :]).then_inc(w_state.sem, 1)
                    mark(("ws0", "ws1")[c])
                    pe.wait_ge(*v_new.at(n, c + 1))
                    for h in range(DH):
                        hs = slice(h * P, (h + 1) * P)
                        mm = pe.matmul(bank[bk][:, hs], tile(A_KDEC)[rows, hs], tile(A_VN)[rows, hs], start=True, stop=True)
                    mm.then_inc(kv_done.sem, 1)
                    for h in range(DH):
                        hs = slice(h * P, (h + 1) * P)
                        pe.matmul(bank[bo][:, hs], tile(A_QDT)[:, hs], state[:, hs], start=True, stop=False)
                        mm = pe.matmul(bank[bo][:, hs], tile(A_QKT)[rows, hs], tile(A_VN)[rows, hs], start=False, stop=True)
                    mm.then_inc(o_done.sem, 1)
                    mark(("kv0", "kv1")[c])
                mark("dn")

                pe.wait_ge(*dn_out.at(n, 1))
                for i in range(2):
                    turn_each(bank[1 + i], o_cat[:, i * 512:(i + 1) * 512]).then_inc(o_T.sem, 1)
                mark("o_T")
                pe.wait_ge(late_in, late)
                pe.wait_ge(*o_copied.at(n, 2))
                ln_row(LN1_G, 0, ln1_rows)
                pe.wait_ge(*o_Tc.at(n, 2))
                ln_row(LN1_B, 1, ln1_rows)
                for c in range(OUT_CHUNKS):
                    tokens_out(n, IN_CHUNKS + c, bank[3 + c // 2][:, (c % 2) * W:(c % 2 + 1) * W], oTv, early)
                    if c % 2:
                        mark(f"out{c // 2}")

                pe.wait_ge(*x1_ready.at(n, 1))
                for i, b in enumerate((5, 0)):
                    turn_each(bank[b], x1[:, i * 512:(i + 1) * 512]).then_inc(x1_T.sem, 1)
                mark("x1_T")
                pe.wait_ge(*x1_Tc.at(n, 2))

                def query_chunks(i):
                    for c in (2 * i, 2 * i + 1):
                        b = bank[1 + i]
                        channels_out(n, IN_CHUNKS + OUT_CHUNKS + c, [b[:, (2 * (c % 2) + j) * P:(2 * (c % 2) + j + 1) * P] for j in range(2)], oTv, early)
                    mark(f"qu{i}")

                def score_keys(i):
                    pe.wait_ge(*queries_c.at(n, i + 1))
                    b = bank[(5, 0, 1, 2)[i]]
                    for j in range(4):
                        l = 4 * i + j
                        mm = pe.matmul(b[:, j * P:(j + 1) * P], arena[:, A_QP * 512 + l * P:A_QP * 512 + (l + 1) * P],
                                       sk[:, l, :], start=True, stop=True)
                    mm.then_inc(key_scores.sem, 1)
                    mark(f"top{i}")
                    mark(f"sel{i}")

                for i in range(4):
                    query_chunks(i)
                    score_keys(i)
                for name in ("pick0", "pick1"):
                    mark(name)

            def experts(n, last):
                for j in range(2 * taken[0], 2 * last):
                    if j == 0:
                        pe.wait_ge(*sums_read.at(n, 0))
                    pe.wait_ge(*gathered[j % RING].at(n, arrived(j)))
                    pe.wait_ge(*diag_ready.at(n, j + 1))
                    for i in range(2):
                        mm = pe.matmul(expert_sum[i][:, :], diag[:, (j % DIAGS) * P:(j % DIAGS + 1) * P],
                                       ring3[:, j % RING, D + i * 512:D + (i + 1) * 512],
                                       start=(j == 0), stop=(j == SLOTS - 1))
                    mm.then_inc(added.sem, 1)
                taken[0] = last

            def second_norm_rows(n):
                pe.wait_ge(*key_scores_c.at(n, 4))
                ln_row(LN2_G, 2, ln2_rows)
                ln_row(LN2_B, 3, ln2_rows)

            taken = [0]
            mix(0, Marks(), early=True)
            with pe.Fori(1, NB) as n:
                taken[0] = 0
                mix(n, Marks(lambda a, b: experts(n - 1, b - 1)))
                second_norm_rows(n)
                experts(n - 1, PAIRS)
            taken[0] = 0
            experts(NB - 1, RING)
            pe.wait_ge(*out_ready.at(NB - 2, 1))
            second_norm_rows(NB - 1)
            experts(NB - 1, PAIRS)

        @block.scalar
        def _(act):
            steps = [0]

            def then(n, ins):
                steps[0] += 1
                ins.then_inc(act_done.sem, 1)
                act.wait_ge(*act_done.at(n, steps[0]))

            act.sem_inc(key_scores_c.sem, 1)
            act.dma_start(positions_in, io["positions"]).then_inc(setup_in, 16)
            act.dma_start(conv_w[:, :], io["conv_w"]).then_inc(setup_in, 16)
            for dst, src in ((neg_a, "a_log"), (dt_b, "dt_bias"), (norm_g, "dn_norm_g"), (sinks, "attn_sinks")):
                act.dma_start(dst[:, :], io[src].partition_broadcast(P)).then_inc(setup_in, 16)
            act.wait_ge(setup_in, setup)
            act.activation(neg_a[:, :], neg_a[:, :], ACT.Exp).then_inc(neg_a_ready, 1)
            act.wait_ge(angles, 1)
            act.activation(sin[:, :], sin[:, :], ACT.Sin).then_inc(tables, 1)
            act.activation(cos[:, :], cos[:, :], ACT.Sin).then_inc(tables, 1)

            def conv_part(n, t):
                act.wait_ge(*chunk_used.at(n, 5 + 2 * t))
                if t == 0:
                    act.wait_ge(*conv_tail.at(n, 0))
                act.copy(conv3[:, DH * t:DH * (t + 1), TAPS - 1:TAPS - 1 + P], by_head(bank[3 + t][:, :])).then_inc(conv_copied.sem, 1)

            def first_taps(n, tiles):
                for t in tiles:
                    act.wait_ge(*conv_copied.at(n, t // DH + 1))
                    act.activation(convo[:, t, :], conv3[:, t, 0:P], ACT.Copy, scale=conv_w[:, t * TAPS:t * TAPS + 1]).then_inc(tap0.sem, 1)

            def mix(n, mark):
                steps[0] = 0
                act.wait_ge(*chosen.at(n, 0))
                act.wait_ge(*chunk_used.at(n, 2))
                act.copy(att[:, 0:512], bank[0][:, :]).then_inc(att_copied.sem, 1)
                mark("q")
                act.wait_ge(*chunk_used.at(n, 3))
                act.copy(att[:, 512:776], bank[1][:, 0:264]).then_inc(att_copied.sem, 1)
                mark("kv")
                act.wait_ge(*gate_pre.at(n, 1))
                act.activation(col(S_EB, DH), att[:, 768:772], ACT.Exp, scale=-1.0)
                then(n, act.activation(col(S_SP, DH), col(S_MN, DH), ACT.Exp))
                act.activation(col(S_SP, DH), col(S_SP, DH), ACT.Ln, bias=1.0).then_inc(gate_exp.sem, 1)
                conv_part(n, 0)
                mark("conv_q")
                act.wait_ge(*att_T.at(n, 1))
                for i in range(2):
                    act.copy(arena[0:HD, (A_QT + i) * 512:(A_QT + i + 1) * 512], bank[i][0:HD, :]).then_inc(att_Tc.sem, 1)
                act.wait_ge(*att_T.at(n, 2))
                act.wait_ge(*att_kept.at(n, 0))
                act.copy(keysT[:, :, P:2 * P], by_head(bank[2][0:HD, 0:2 * P], KV)).then_inc(att_Tc.sem, 1)
                mark("turn_qk")
                conv_part(n, 1)
                first_taps(n, range(DH))
                mark("conv_k")
                conv_part(n, 2)
                first_taps(n, range(DH, 2 * DH))
                mark("conv_v")
                act.wait_ge(*chunk_used.at(n, IN_CHUNKS))
                act.copy(z[:, :], bank[2][:, :]).then_inc(z_copied.sem, 1)
                first_taps(n, range(2 * DH, 3 * DH))
                mark("z")
                mark("scores")
                act.wait_ge(*neg_max.at(n, 1))
                for h in range(HEADS):
                    pr = arena[:, A_P * 512 + h * 2 * P:A_P * 512 + (h + 1) * 2 * P]
                    act.activation(pr, pr, ACT.Exp, bias=col(S_NMAX + h), accum_out=col(S_SUM + h)).then_inc(probs.sem, 1)
                act.activation(col(S_SNK, HEADS), col(S_SNK, HEADS), ACT.Exp).then_inc(probs.sem, 1)
                mark("softmax")
                for i in range(4):
                    act.wait_ge(*probs_T.at(n, i + 1))
                    act.copy(tile(A_PT + i), bank[i][:, :]).then_inc(probs_Tc.sem, 1)
                mark("turn_p")
                act.wait_ge(*conv_step.at(n, 3 * DH * (TAPS - 1)))
                then(n, act.activation(conv[:, :], conv[:, :], ACT.Silu))
                act.activation(z[:, :], z[:, :], ACT.Silu).then_inc(silu_done.sem, 1)
                act.activation(tile(A_SQ, 2), conv[:, 0:2 * 512], ACT.Square).then_inc(squares.sem, 1)
                mark("att_o")
                act.wait_ge(*att_o.at(n, 1))
                act.copy(keysT[:, :, 0:P], keysT[:, :, P:2 * P])
                act.copy(vrows[:, 0, :], vrows[:, 1, :]).then_inc(att_kept.sem, 1)
                act.wait_ge(*norms.at(n, 2))
                for i in range(2):
                    ins = act.activation(tile(A_SQ + i), bank[2 + i][:, :], ACT.Ln, bias=C["eps_l2"])
                then(n, ins)
                act.activation(tile(A_SQ), tile(A_SQ), ACT.Exp, scale=-0.5, bias=C["ln_qscale"])
                act.activation(tile(A_SQ + 1), tile(A_SQ + 1), ACT.Exp, scale=-0.5).then_inc(inv_norms.sem, 1)
                act.wait_ge(*g_sums.at(n, 2))
                then(n, act.copy(col(S_GC, 2 * DH), bank[1][:, 0:2 * DH]))
                act.activation(col(S_EGC, DH), col(S_GC, DH), ACT.Exp).then_inc(gc_copied.sem, 1)
                act.activation(tile(A_EG), bank[0][:, :], ACT.Exp).then_inc(gc_copied.sem, 1)
                mark("norms")
                act.wait_ge(*diffs.at(n, 1))
                act.activation(tile(A_DI), tile(A_DI), ACT.Exp, scale=-1.0).then_inc(decays.sem, 1)
                act.wait_ge(*diffs.at(n, 2))
                act.activation(tile(A_DT), tile(A_DT), ACT.Exp).then_inc(decays.sem, 1)
                act.wait_ge(*kd_pre.at(n, 1))
                act.activation(col(S_KD, DH), col(S_KD, DH), ACT.Exp).then_inc(kd_exp.sem, 1)
                mark("decay")
                mark("kk")
                mark("aT")
                for k, (dst, b) in enumerate(((A_N2, 1), (A_N2T, 3), (A_N4, 4), (A_N4T, 5), (A_N8, 1))):
                    act.wait_ge(*sq.at(n, k + 1))
                    act.copy(tile(dst), bank[b][:, :]).then_inc(sq_copied.sem, 1)
                    if k in (1, 3, 4):
                        mark({1: "pow2", 3: "pow4", 4: "pow8"}[k])
                mark("prod3")
                for k, (dst, b) in enumerate(((A_Z, 5), (A_TT, 0), (A_Z, 3), (A_TT, 4))):
                    act.wait_ge(*turn.at(n, k + 1))
                    act.copy(tile(dst), bank[b][:, :]).then_inc(turn_copied.sem, 1)
                    if k % 2:
                        mark(("turn32", "turn64")[k // 2])
                        mark(("merge32", "merge64")[k // 2])
                for k, (dst, b) in enumerate(((A_U, 0), (A_WT, 1))):
                    act.wait_ge(*solved.at(n, k + 1))
                    act.copy(tile(dst), bank[b][:, :]).then_inc(solved_copied.sem, 1)
                mark("solve")
                for c, b in enumerate((2, 0)):
                    rows = slice(c * CHUNK, (c + 1) * CHUNK)
                    mark(("ws0", "ws1")[c])
                    act.wait_ge(*o_done.at(n, c + 1))
                    act.copy(tile(A_O)[rows, :], bank[b][rows, :]).then_inc(o_copied.sem, 1)
                    mark(("kv0", "kv1")[c])
                act.wait_ge(*o_ms.at(n, 1))
                then(n, act.activation(col(S_RT, DH), col(S_SS, DH), ACT.Ln, bias=C["eps_rms"]))
                act.activation(col(S_RT, DH), col(S_RT, DH), ACT.Exp, scale=-0.5).then_inc(root.sem, 1)
                mark("dn")
                for i in range(2):
                    act.wait_ge(*o_T.at(n, i + 1))
                    act.copy(oT[:, i * 512:(i + 1) * 512], bank[1 + i][:, :]).then_inc(o_Tc.sem, 1)
                mark("o_T")
                mark("out0")
                act.wait_ge(*var_ready.at(n, 1))
                then(n, act.activation(col(S_LN1), col(S_LN1 + 3), ACT.Ln, bias=C["eps_ln"]))
                act.activation(col(S_LN1), col(S_LN1), ACT.Exp, scale=-0.5).then_inc(root.sem, 1)
                mark("out1")
                for i, b in enumerate((5, 0)):
                    act.wait_ge(*x1_T.at(n, i + 1))
                    act.copy(oT[:, i * 512:(i + 1) * 512], bank[b][:, :]).then_inc(x1_Tc.sem, 1)
                mark("x1_T")

                def queries_out(i):
                    act.wait_ge(*chunk_used.at(n, IN_CHUNKS + OUT_CHUNKS + 2 * (i + 1)))
                    act.copy(tile(A_QP + i), bank[1 + i][:, :]).then_inc(queries_c.sem, 1)
                    mark(f"qu{i}")

                def key_scores_out(i):
                    act.wait_ge(*key_scores.at(n, i + 1))
                    act.copy(tile(A_S + i), bank[(5, 0, 1, 2)[i]][:, :]).then_inc(key_scores_c.sem, 1)
                    mark(f"top{i}")
                    mark(f"sel{i}")

                for i in range(4):
                    queries_out(i)
                    key_scores_out(i)
                act.wait_ge(*best_sub.at(n, 1))
                act.activation(gate[:, :], gate[:, :], ACT.Exp).then_inc(best_exp.sem, 1)
                mark("pick0")
                mark("pick1")

            def experts(n, first, last):
                if first == 0:
                    act.wait_ge(*rows_staged.at(n, 1))
                for q in range(first, last):
                    pair = (2 * q, 2 * q + 1)
                    act.wait_ge(*dotted.at(n, 2 * q + 2))
                    act.activation(h_raw[:, pair[0]:pair[1] + 1], h_raw[:, pair[0]:pair[1] + 1], ACT.Gelu).then_inc(gelued.sem, 1)
                    act.wait_ge(*gelued.at(n, q + 1))
                    for j in pair:
                        act.activation(h_w[:, j:j + 1], h_raw[:, j:j + 1], ACT.Copy, scale=gate_used[:, j:j + 1]).then_inc(weighted.sem, 1)
                    for j in pair:
                        act.wait_ge(*weighted.at(n, j + 1))
                        act.wait_ge(*added.at(n, j - DIAGS + 1))
                        act.activation(diag[:, (j % DIAGS) * P:(j % DIAGS + 1) * P], C["ident"], ACT.Copy,
                                       scale=h_w[:, j:j + 1]).then_inc(diag_ready.sem, 1)

            def finish(n):
                act.wait_ge(*var_out.at(n, 1))
                act.activation(col(S_OUT), col(S_OUT + 3), ACT.Ln, bias=C["eps_ln"]).then_inc(act_out_done.sem, 1)
                act.wait_ge(*act_out_done.at(n, 1))
                act.activation(col(S_OUT), col(S_OUT), ACT.Exp, scale=-0.5).then_inc(root_out.sem, 1)
                act.wait_ge(*out_ready.at(n, 1))
                act.dma_start(io["out"][bass.ds(n, 1), :, :].rearrange("n p c -> (n p) c"), o_cat[:, :]).then_inc(stored.sem, 16)

            def late_loads():
                act.dma_start(sub_keys[:, :], io["sub_keys"]).then_inc(late_in, 16)
                act.dma_start(k_keys[LN_ROWS, :], io["ln_rows"]).then_inc(late_in, 16)

            mix(0, Marks(behind={"z": late_loads}))
            with act.Fori(1, NB) as n:
                marks = Marks(lambda a, b: experts(n - 1, a, b))
                mix(n, marks)
                experts(n - 1, marks.done, PAIRS)
                finish(n - 1)
            experts(NB - 1, 0, PAIRS)
            finish(NB - 1)
            assert steps[0] == ACT_STEPS, steps

        @block.vector
        def _(dve):
            steps = [0]
            setup_step = setup_steps

            def then(n, ins):
                steps[0] += 1
                ins.then_inc(dve_done.sem, 1)
                dve.wait_ge(*dve_done.at(n, steps[0]))

            count = [0]

            def first(ins):
                count[0] += 1
                ins.then_inc(setup_step, 1)
                dve.wait_ge(setup_step, count[0])

            tt, ts, stt = dve.tensor_tensor, dve.tensor_scalar, dve.scalar_tensor_tensor

            dve.memset(state[:, :], 0.0).then_inc(state_new.sem, 1)
            dve.memset(k_keys[0:HD, :], 0.0)
            dve.memset(v_rows[:, :], 0.0).then_inc(att_kept.sem, 1)
            dve.memset(conv_in[:, :], 0.0).then_inc(conv_tail.sem, 1)
            for unused in (rows_staged, sums_read, chosen, out_ready):
                dve.sem_inc(unused.sem, unused.before)
            dve.wait_ge(setup_in, setup)
            first(dve.tensor_copy(mask[:, P:2 * P], C["band"][:, P:2 * P]))
            first(dve.memset(mask[:, 0:P], NEG))
            pos = small[:, 0:NB]
            c3 = lambda t: t[:, :].rearrange("p (n c) -> p n c", n=NB)
            turns_i = arena[:, 512:512 + NB * HALF].bitcast(I32)
            turns = arena[:, 1024:1024 + NB * HALF]
            over = arena[:, 1536:1536 + NB * HALF]
            first(dve.tensor_copy(pos, positions_in))
            first(tt(c3(sin), over_cols(pos, HALF), over_heads(C["freq"], NB), ALU.mult))
            first(ts(turns, sin[:, :], 1.0 / (2 * math.pi), None, ALU.mult))
            first(dve.tensor_copy(turns_i, turns))
            first(dve.tensor_copy(turns, turns_i))
            for part in TWO_PI:
                first(stt(out=sin[:, :], in0=turns, scalar=-part, in1=sin[:, :], op0=ALU.mult, op1=ALU.add))

            def wrap(t):
                for op, edge, shift in ((ALU.is_gt, math.pi, -2 * math.pi), (ALU.is_lt, -math.pi, 2 * math.pi)):
                    first(ts(over, t[:, :], edge, shift, op, ALU.mult))
                    first(tt(t[:, :], t[:, :], over, ALU.add))
            wrap(sin)
            first(ts(cos[:, :], sin[:, :], math.pi / 2, None, ALU.add))
            wrap(cos)
            first(ts(sin[:, :], sin[:, :], 3.1415925, -3.1415925, ALU.min, ALU.max))
            ts(cos[:, :], cos[:, :], 3.1415925, -3.1415925, ALU.min, ALU.max).then_inc(angles, 1)
            dve.wait_ge(neg_a_ready, 1)
            first(ts(neg_a[:, :], neg_a[:, :], -1.0, None, ALU.mult))
            dve.wait_ge(tables, 2)

            def refine(then, y, v, eps, t):
                then(tt(t, y, y, ALU.mult))
                then(stt(out=t, in0=v, scalar=eps, in1=t, op0=ALU.add, op1=ALU.mult))
                then(ts(t, t, -0.5, 1.5, ALU.mult, ALU.add))
                then(tt(y, y, t, ALU.mult))

            def layer_norm(then, x, g, b, g_there, b_there, out, at, var, rooted):
                bn = small[:, at + 4:at + 16].rearrange("p (a c) -> p a c", a=2)
                for i in range(2):
                    ins = dve.bn_stats(bn[:, i, :], x[:, i * 512:(i + 1) * 512])
                then(ins)
                alone(dve)
                dve.bn_aggr(col(at + 2, 2), small[:, at + 4:at + 16]).then_inc(var.sem, 1)
                dve.wait_ge(*rooted)
                refine(then, col(at), col(at + 3), LN_EPS, col(at + 1))
                then(ts(x[:, :], x[:, :], col(at + 2), col(at), ALU.subtract, ALU.mult))
                halves = [slice(i * 512, (i + 1) * 512) for i in range(2)]
                dve.wait_ge(*g_there)
                for i, half in enumerate(halves):
                    ins = tt(x[:, half], x[:, half], g[i][:, :], ALU.mult)
                then(ins)
                dve.wait_ge(*b_there)
                for i, half in enumerate(halves):
                    ins = tt(out[:, half], x[:, half], b[i][:, :], ALU.add)
                return ins

            bv = best_v.rearrange("p (h s k) -> p h s k", s=2, k=TOPK)
            bi = best_if.rearrange("p (h s k) -> p h s k", s=2, k=TOPK)
            hot = arena[:, A_HOT * 512:(A_HOT + 4) * 512].rearrange("p (h k i) -> p h k i", h=PH, k=TOPK)
            tv = top_v.rearrange("p (h k) -> p h k", h=PH)
            gt = gate[:, :].rearrange("p (h k) -> p h k", h=PH)

            def sixteen_best(n, values, numbers, sources, k):
                lists = [(slice((k + i) * TOPK, (k + i) * TOPK + 8), slice((k + i) * TOPK + 8, (k + i + 1) * TOPK), source)
                         for i, source in enumerate(sources)]

                def maxima(part):
                    for one in lists:
                        ins = dve.max(values[:, one[part]], one[2])
                    then(n, ins)
                    alone(dve)

                alone(dve)
                maxima(0)
                for a, b, source in lists:
                    dve.max_index(numbers[:, a], values[:, a], source)
                for a, b, source in lists:
                    ins = dve.match_replace(source, values[:, a], source, LOWEST)
                then(n, ins)
                alone(dve)
                maxima(1)
                for a, b, source in lists:
                    ins = dve.max_index(numbers[:, b], values[:, b], source)
                return ins

            def conv_taps(n, k):
                for t in range(3 * DH):
                    if k == 1:
                        dve.wait_ge(*tap0.at(n, t + 1))
                    else:
                        dve.wait_ge(*conv_step.at(n, (k - 2) * 3 * DH + t + 1))
                    stt(out=convo[:, t, :], in0=conv3[:, t, k:k + P], scalar=conv_w[:, t * TAPS + k:t * TAPS + k + 1],
                        in1=convo[:, t, :], op0=ALU.mult, op1=ALU.add).then_inc(conv_step.sem, 1)

            def mix(n, mark):
                steps[0] = 0
                mark("q")
                dve.wait_ge(*att_copied.at(n, 2))
                then(n, tt(col(S_AX, DH), att[:, 772:776], dt_b[:, :], ALU.add))
                then(n, ts(col(S_NX, DH), col(S_AX, DH), -1.0, None, ALU.mult))
                tt(col(S_MN, DH), col(S_AX, DH), col(S_NX, DH), ALU.min).then_inc(gate_pre.sem, 1)
                qk = att[:, 0:640].rearrange("p (h c) -> p h c", c=HD)
                cs = cos[:, bass.ts(n, HALF)].unsqueeze(1).to_broadcast([P, HEADS + KV, HALF])
                sn = sin[:, bass.ts(n, HALF)].unsqueeze(1).to_broadcast([P, HEADS + KV, HALF])
                x_lo, x_hi = qk[:, :, 0:HALF], qk[:, :, HALF:HD]
                tt(rtmp[0], x_lo, cs, ALU.mult)
                tt(rtmp[1], x_hi, sn, ALU.mult)
                tt(rtmp[2], x_hi, cs, ALU.mult)
                then(n, tt(rtmp[3], x_lo, sn, ALU.mult))
                tt(rot[:, :, 0:HALF], rtmp[0], rtmp[1], ALU.subtract).then_inc(roped.sem, 1)
                tt(rot[:, :, HALF:HD], rtmp[2], rtmp[3], ALU.add).then_inc(roped.sem, 1)
                dve.wait_ge(*att_kept.at(n, 0))
                dve.tensor_copy(vrows[:, 1, :], att[:, 640:768])
                mark("kv")
                dve.wait_ge(*gate_exp.at(n, 1))
                then(n, ts(col(S_EB, DH), col(S_EB, DH), 1.0, None, ALU.add))
                then(n, dve.reciprocal(col(S_BETA, DH), col(S_EB, DH)))
                then(n, ts(col(S_AX, DH), col(S_AX, DH), 0.0, None, ALU.max))
                then(n, tt(col(S_SP, DH), col(S_SP, DH), col(S_AX, DH), ALU.add))
                tt(col(S_G, DH), col(S_SP, DH), neg_a[:, :], ALU.mult).then_inc(g_ready.sem, 1)
                mark("conv_q")
                mark("turn_qk")
                mark("conv_k")
                mark("conv_v")
                conv_taps(n, 1)
                mark("z")
                for i in range(4):
                    dve.wait_ge(*scored.at(n, i + 1))
                    stt(out=by_head(tile(A_P + i), 2), in0=by_head(bank[2 + i][:, :], 2), scalar=HD ** -0.5,
                        in1=over_heads(mask[:, :], 2), op0=ALU.mult, op1=ALU.add).then_inc(masked.sem, 1)
                dve.wait_ge(*masked.at(n, 4))
                then(n, dve.tensor_reduce(col(S_MAX, HEADS), arena[:, A_P * 512:(A_P + 4) * 512].rearrange("p (h c) -> p h c", h=HEADS),
                                          AX.X, ALU.max))
                then(n, tt(col(S_MAX, HEADS), col(S_MAX, HEADS), sinks[:, :], ALU.max))
                tt(col(S_SNK, HEADS), sinks[:, :], col(S_MAX, HEADS), ALU.subtract)
                ts(col(S_NMAX, HEADS), col(S_MAX, HEADS), -1.0, None, ALU.mult).then_inc(neg_max.sem, 1)
                dve.tensor_copy(mask[:, 0:P], C["band"][:, 0:P])
                mark("scores")
                conv_taps(n, 2)
                conv_taps(n, 3)
                dve.tensor_copy(conv3[:, :, 0:TAPS - 1], conv3[:, :, P:P + TAPS - 1]).then_inc(conv_tail.sem, 1)
                mark("softmax")
                dve.wait_ge(*probs.at(n, 9))
                then(n, tt(col(S_DEN, HEADS), col(S_SUM, HEADS), col(S_SNK, HEADS), ALU.add))
                then(n, dve.reciprocal(col(S_RIN, HEADS), col(S_DEN, HEADS)))
                mark("turn_p")
                dve.wait_ge(*probs_T.at(n, 4))
                dve.wait_ge(*g_ready.at(n, 1))
                tt(by_head(tile(A_UG)), over_heads(C["upto"], DH), over_cols(col(S_G, DH), P), ALU.mult).then_inc(g_ready.sem, 1)
                dve.wait_ge(*att_o.at(n, 1))
                dve.wait_ge(*stored.at(n, -16))
                tt(o_cat[:, 0:512].rearrange("p (h c) -> p h c", h=HEADS), bank[4][:, :].rearrange("p (h c) -> p h c", h=HEADS),
                   over_cols(col(S_RIN, HEADS), HD), ALU.mult).then_inc(att_out.sem, 1)
                mark("att_o")
                mark("norms")
                dve.wait_ge(*gc_copied.at(n, 2))
                then(n, tt(by_head(tile(A_DD)), by_head(bank[0][:, :]), over_cols(col(S_GC, DH), P), ALU.subtract))
                ts(tile(A_DI), tile(A_DD), 0.0, None, ALU.max).then_inc(diffs.sem, 1)
                ts(tile(A_DT), tile(A_DD), 0.0, None, ALU.min).then_inc(diffs.sem, 1)
                tt(col(S_BG, DH), col(S_BETA, DH), col(S_EGC, DH), ALU.mult)
                tt(col(S_KD, DH), col(S_GL, DH), col(S_GC, DH), ALU.subtract).then_inc(kd_pre.sem, 1)
                dve.wait_ge(*inv_norms.at(n, 1))
                tt(conv[:, 0:1024], conv[:, 0:1024], tile(A_SQ, 2), ALU.mult).then_inc(qk_normed.sem, 1)
                mark("decay")
                dve.wait_ge(*decays.at(n, 1))
                then(n, tt(by_head(tile(A_DI)), by_head(tile(A_DI)), over_heads(C["strict"], DH), ALU.mult))
                then(n, tt(by_head(tile(A_DI)), by_head(tile(A_DI)), over_cols(col(S_BETA, DH), P), ALU.mult))
                dve.wait_ge(*ktok.at(n, 2))
                tt(tile(A_A), bank[5][:, :], tile(A_DI), ALU.mult).then_inc(a_ready.sem, 1)
                dve.wait_ge(*a_ready.at(n, 1))
                tt(by_head(tile(A_N)), by_head(tile(A_A)), over_heads(C["same16"], DH), ALU.mult)
                dve.wait_ge(*kd_exp.at(n, 1))
                dve.wait_ge(*ktok.at(n, 1))
                tt(by_head(tile(A_KBG)), by_head(bank[3][:, :]), over_cols(col(S_BG, DH), P), ALU.mult).then_inc(scaled.sem, 1)
                tt(by_head(tile(A_KDEC)), by_head(bank[3][:, :]), over_cols(col(S_KD, DH), P), ALU.mult).then_inc(scaled.sem, 1)
                mark("kk")
                dve.wait_ge(*aT.at(n, 1))
                tt(by_head(tile(A_NT)), by_head(bank[0][:, :]), over_heads(C["same16"], DH), ALU.mult).then_inc(nT_ready.sem, 1)
                dve.wait_ge(*nT_ready.at(n, 1))
                stt(out=by_head(tile(A_R)), in0=by_head(tile(A_NT)), scalar=-1.0, in1=over_heads(C["ident"], DH),
                    op0=ALU.mult, op1=ALU.add).then_inc(x0_ready.sem, 1)
                dve.wait_ge(*ktok.at(n, 3))
                tt(by_head(tile(A_VB)), by_head(bank[4][:, :]), over_cols(col(S_BETA, DH), P), ALU.mult).then_inc(scaled.sem, 1)
                mark("aT")
                tt(by_head(tile(A_E32)), by_head(tile(A_A)), over_heads(C["off32"], DH), ALU.mult)
                tt(by_head(tile(A_E64)), by_head(tile(A_A)), over_heads(C["off64"], DH), ALU.mult)
                dve.wait_ge(*decays.at(n, 2))
                then(n, tt(by_head(tile(A_DT)), by_head(tile(A_DT)), over_heads(C["upto"], DH), ALU.mult))
                mark("pow2")
                dve.wait_ge(*prod.at(n, 1))
                tt(tile(A_R), tile(A_R), bank[0][:, :], ALU.add).then_inc(prod_added.sem, 1)
                dve.wait_ge(*ktok.at(n, 4))
                tt(tile(A_QKT), bank[2][:, :], tile(A_DT), ALU.mult).then_inc(scaled.sem, 1)
                tt(tile(A_QDT), conv[:, 0:512], tile(A_EG), ALU.mult).then_inc(scaled.sem, 1)
                mark("pow4")
                for k, b, name in ((1, 3, "pow8"), (2, 4, "prod3")):
                    dve.wait_ge(*prod.at(n, k + 1))
                    dve.wait_ge(*prod_added.at(n, k))
                    tt(tile(A_R), tile(A_R), bank[b][:, :], ALU.add).then_inc(prod_added.sem, 1)
                    mark(name)
                for m, b in enumerate((1, 5)):
                    mark(("turn32", "turn64")[m])
                    dve.wait_ge(*merge.at(n, m + 1))
                    tt(tile(A_R), tile(A_R), bank[b][:, :], ALU.subtract).then_inc(merged.sem, 1)
                    mark(("merge32", "merge64")[m])
                mark("solve")
                for c, (bw, bk) in enumerate(((3, 4), (5, 1))):
                    rows = slice(c * CHUNK, (c + 1) * CHUNK)
                    dve.wait_ge(*solved_copied.at(n, 1))
                    dve.wait_ge(*w_state.at(n, c + 1))
                    tt(tile(A_VN)[rows, :], tile(A_U)[rows, :], bank[bw][rows, :], ALU.subtract).then_inc(v_new.sem, 1)
                    mark(("ws0", "ws1")[c])
                    dve.wait_ge(*kv_done.at(n, c + 1))
                    dve.wait_ge(*o_done.at(n, c + 1))
                    last = (c + 1) * CHUNK - 1
                    for h in range(DH):
                        hs = slice(h * P, (h + 1) * P)
                        ins = stt(out=state[:, hs], in0=state[:, hs], scalar=tile(A_EG)[:, h * P + last:h * P + last + 1],
                                  in1=bank[bk][:, hs], op0=ALU.mult, op1=ALU.add)
                    ins.then_inc(state_new.sem, 1)
                    mark(("kv0", "kv1")[c])
                dve.wait_ge(*o_copied.at(n, 2))
                then(n, tt(tile(A_DI), tile(A_O), tile(A_O), ALU.mult))
                then(n, dve.tensor_reduce(col(S_SS, DH), by_head(tile(A_DI)), AX.X, ALU.add))
                ts(col(S_SS, DH), col(S_SS, DH), 1.0 / DK, None, ALU.mult).then_inc(o_ms.sem, 1)
                then(n, tt(by_head(tile(A_O)), by_head(tile(A_O)), over_heads(norm_g[:, :], DH), ALU.mult))
                dve.wait_ge(*silu_done.at(n, 1))
                then(n, tt(tile(A_O), tile(A_O), z[:, :], ALU.mult))
                dve.wait_ge(*root.at(n, 1))
                refine(lambda ins: then(n, ins), col(S_RT, DH), col(S_SS, DH), RMS_EPS, col(S_RT + 4, DH))
                tt(by_head(o_cat[:, 512:1024]), by_head(tile(A_O)), over_cols(col(S_RT, DH), P), ALU.mult).then_inc(dn_out.sem, 1)
                mark("dn")
                mark("o_T")
                dve.wait_ge(*x_loaded.at(n, 16))
                for i in range(2):
                    dve.wait_ge(*chunk_used.at(n, IN_CHUNKS + 2 * (i + 1)))
                    ins = stt(out=x1[:, i * 512:(i + 1) * 512], in0=x1[:, i * 512:(i + 1) * 512], scalar=ALPHA,
                              in1=bank[3 + i][:, :], op0=ALU.mult, op1=ALU.add)
                    if i == 0:
                        mark("out0")
                ins.then_inc(residual.sem, 1)
                dve.wait_ge(*residual.at(n, 1))
                layer_norm(lambda ins: then(n, ins), x1, LN1_G, LN1_B, ln1_rows.at(n, 1), ln1_rows.at(n, 2), x1, S_LN1, var_ready, root.at(n, 2)).then_inc(x1_ready.sem, 1)
                mark("out1")
                mark("x1_T")
                for i in range(4):
                    mark(f"qu{i}")
                    dve.wait_ge(*key_scores_c.at(n, i + 1))
                    then(n, sixteen_best(n, best_v, best_i, [arena[:, A_S * 512 + l * KEYS:A_S * 512 + (l + 1) * KEYS] for l in range(4 * i, 4 * i + 4)], 4 * i))
                    if i == 3:
                        dve.tensor_copy(best_if, best_i)
                    mark(f"top{i}")
                    pair = (2 * i, 2 * i + 1)
                    cands = [arena[:, A_CAND * 512 + h * 256:A_CAND * 512 + (h + 1) * 256] for h in pair]
                    for h, cd in zip(pair, cands):
                        ins = tt(cd.rearrange("p (a b) -> p a b", a=TOPK), bv[:, h, 0, :].unsqueeze(2).to_broadcast([P, TOPK, TOPK]),
                                 bv[:, h, 1, :].unsqueeze(1).to_broadcast([P, TOPK, TOPK]), ALU.add)
                    then(n, ins)
                    ins = sixteen_best(n, top_v, top_p, cands, 2 * i)
                    if i == 3:
                        then(n, ins)
                        tt(gt, tv, tv[:, :, 0:1].to_broadcast([P, PH, TOPK]), ALU.subtract).then_inc(best_sub.sem, 1)
                    mark(f"sel{i}")
                then(n, ts(pos_u, top_p, 4, None, ALU.logical_shift_right))
                then(n, dve.tensor_copy(pos_hi, pos_u))
                then(n, ts(pos_u, top_p, TOPK - 1, None, ALU.bitwise_and))
                then(n, dve.tensor_copy(pos_lo, pos_u))
                for side, pos_s in enumerate((pos_hi, pos_lo)):
                    for h in range(PH):
                        ph = pos_s[:, h * TOPK:(h + 1) * TOPK]
                        ins = tt(hot[:, h], over_heads(C["iota"], TOPK), over_cols(ph, TOPK), ALU.is_equal)
                    then(n, ins)
                    for h in range(PH):
                        ins = tt(hot[:, h], hot[:, h], bi[:, h, side, :].unsqueeze(1).to_broadcast([P, TOPK, TOPK]), ALU.mult)
                    then(n, ins)
                    then(n, dve.tensor_reduce(pos_s, hot.rearrange("p h k i -> p (h k) i"), AX.X, ALU.add))
                    if side == 0:
                        mark("pick0")
                then(n, stt(out=pos_hi, in0=pos_hi, scalar=float(KEYS), in1=pos_lo, op0=ALU.mult, op1=ALU.add))
                dve.tensor_copy(expert[:, :], pos_hi).then_inc(chosen.sem, 1)
                dve.wait_ge(*best_exp.at(n, 1))
                then(n, dve.tensor_reduce(col(S_GS, PH), gt, AX.X, ALU.add))
                then(n, dve.reciprocal(col(S_GR, PH), col(S_GS, PH)))
                tt(gt, gt, over_cols(col(S_GR, PH), TOPK), ALU.mult).then_inc(chosen.sem, 1)
                mark("pick1")

            def stage_experts(n, part):
                s = slice(0, STAGED) if part == 0 else slice(STAGED, SLOTS)
                dve.wait_ge(*chosen.at(n, 1))
                dve.tensor_copy(expert_used[:, s], expert[:, s]).then_inc(staged.sem, 1)

            def stage_rows(n):
                dve.wait_ge(*chosen.at(n, 2))
                dve.tensor_copy(gate_used[:, :], gate[:, :])
                dve.tensor_copy(x1_used[:, :], x1[:, :]).then_inc(rows_staged.sem, 1)

            def experts(n, first, last):
                if first == 0:
                    dve.wait_ge(*rows_staged.at(n, 1))
                for q in range(first, last):
                    for j in (2 * q, 2 * q + 1):
                        dve.wait_ge(*gathered[j % RING].at(n, arrived(j)))
                        u = ring3[:, j % RING, 0:D]
                        dve.tensor_tensor_reduce(u, u, x1_used[:, :], 1.0, 0.0, ALU.mult, ALU.add, h_raw[:, j:j + 1]).then_inc(dotted.sem, 1)

            def finish(n):
                done = [0]

                def then_out(ins):
                    done[0] += 1
                    ins.then_inc(dve_out_done.sem, 1)
                    dve.wait_ge(*dve_out_done.at(n, done[0]))

                dve.wait_ge(*added.at(n, SLOTS))
                for i in range(2):
                    ins = stt(out=x1_used[:, i * 512:(i + 1) * 512], in0=x1_used[:, i * 512:(i + 1) * 512], scalar=ALPHA,
                              in1=expert_sum[i][:, :], op0=ALU.mult, op1=ALU.add)
                ins.then_inc(sums_read.sem, 1)
                dve.wait_ge(*sums_read.at(n, 1))
                dve.wait_ge(*stored.at(n, 0))
                layer_norm(then_out, x1_used, LN2_G, LN2_B, ln2_rows.at(n, 1), ln2_rows.at(n, 2), o_cat, S_OUT, var_out, root_out.at(n, 1)).then_inc(out_ready.sem, 1)
                dve.wait_ge(*out_ready.at(n, 1))
                assert done[0] == LN_STEPS, done

            mix(0, Marks())
            assert steps[0] == DVE_STEPS, steps
            stage_experts(0, 0)
            stage_experts(0, 1)
            stage_rows(0)
            with dve.Fori(1, NB) as n:
                marks = Marks(lambda a, b: experts(n - 1, a, b))
                mix(n, marks)
                stage_experts(n, 0)
                experts(n - 1, marks.done, PAIRS)
                stage_experts(n, 1)
                finish(n - 1)
                stage_rows(n)
            experts(NB - 1, 0, PAIRS)
            finish(NB - 1)


def chunked(w):
    d, m = w.shape
    return np.ascontiguousarray(w.reshape(d // P, P, m // W, W).transpose(2, 1, 0, 3)).reshape(m // W, P, -1)


def by_partition(a):
    return np.ascontiguousarray(a.reshape(-1, P, a.shape[1]).transpose(1, 0, 2)).reshape(P, -1)


def kernel(**inputs):
    import concourse.bacc as bacc
    from concourse.bass_utils import run_bass_kernel_spmd

    a = {k: np.asarray(v) for k, v in inputs.items()}
    x = a["x"].reshape(SEQ, D)
    w_in = a["w_in"]
    qkv, dn = HEADS * HD + 2 * KV * HD, DH * DK
    b_at = qkv + 3 * dn
    z_at = b_at + 2 * DH
    w_main = np.concatenate([w_in[:, :b_at], w_in[:, z_at:]], axis=1)
    arrays = {
        "consts": constants(),
        "weights": np.concatenate([chunked(w_main), chunked(a["w_out"]), chunked(a["peer_w_query"])], axis=0),
        "w_ba": by_partition(w_in[:, b_at:z_at]),
        "sub_keys": np.ascontiguousarray(a["peer_sub_keys"].transpose(3, 0, 1, 2)).reshape(P, -1),
        "conv_w": np.ascontiguousarray(a["conv_w"].reshape(TAPS, 3 * DH, P).transpose(2, 1, 0)).reshape(P, -1),
        "xT": np.ascontiguousarray(x.reshape(NB, P, KT, P).transpose(0, 3, 2, 1)).reshape(NB, P, D),
        "x": x.reshape(NB, P, D),
        "positions": np.ascontiguousarray(a["positions"].reshape(NB, P).T.astype(np.int32)),
        "ln_rows": np.stack([a[k] for k in ("ln1_g", "ln1_b", "ln2_g", "ln2_b")]).reshape(8, D // 2),
        "uv": np.concatenate([a["peer_u"], a["peer_v"]], axis=1),
    }
    for k in ("a_log", "dt_bias", "dn_norm_g", "attn_sinks"):
        arrays[k] = a[k]
    nc = bacc.Bacc("TRN2", target_bir_lowering=False, num_devices=1)
    io = {k: nc.dram_tensor(f"in_{k}", v.shape, mybir.dt.from_np(v.dtype), kind="ExternalInput").ap() for k, v in arrays.items()}
    io["out"] = nc.dram_tensor("out_0", (NB, P, D), F32, kind="ExternalOutput").ap()
    build(nc, io)
    r = run_bass_kernel_spmd(nc, [{f"in_{k}": v for k, v in arrays.items()}], core_ids=[0])
    return r.results[0]["out_0"].reshape(1, SEQ, D)
```
